# Optimizing a Trainium2 kernel written in Bass

```python
import jax, jax.numpy as jnp
from jax import lax
import numpy as np

D_MODEL = 1024
BATCH = 1
SEQ = 512
DEPTH = 1

CHUNK = 64
Q_BLOCK = 2 * CHUNK
MIX_WIDTH = D_MODEL
POOL_WIDTH = MIX_WIDTH // 2
POOL_WINDOWS = (2, 4, 8, 16)
POOL_GROUP = POOL_WIDTH // len(POOL_WINDOWS)
ATTN_WIDTH = MIX_WIDTH - POOL_WIDTH
ATTN_HEADS = 8
HEAD_DIM = ATTN_WIDTH // ATTN_HEADS
IN_WIDTH = POOL_WIDTH + 3 * ATTN_WIDTH + ATTN_HEADS
PEER_HEADS = 8
PEER_KEYS = 128
PEER_EXPERTS = PEER_KEYS * PEER_KEYS
PEER_QUERY = 256
PEER_TOPK = 16
PEER_TOKEN_BLOCK = 128
EPS = 1e-6

kernel_name = "hybrid_pool_fox_peer_block"

def rms_norm(x, g):
    xf = x.astype(jnp.float32)
    y = xf * lax.rsqrt(jnp.mean(xf * xf, axis=-1, keepdims=True) + EPS)
    return (y * g.astype(jnp.float32)).astype(x.dtype)

def pool_mixer(p, w_pool, pool_scale):
    B, S, _ = p.shape
    pf = p.astype(jnp.float32)
    cs = jnp.cumsum(pf, axis=1)
    cs = jnp.concatenate([jnp.zeros_like(cs[:, :1]), cs], axis=1)
    t = jnp.arange(S)
    outs = []
    for gi, w in enumerate(POOL_WINDOWS):
        sl = slice(gi * POOL_GROUP, (gi + 1) * POOL_GROUP)
        start = jnp.maximum(t + 1 - w, 0)
        win_sum = cs[:, 1:, sl] - cs[:, start, sl]
        cnt = (t + 1 - start).astype(jnp.float32)[None, :, None]
        outs.append(win_sum / cnt - pf[:, :, sl])
    pooled = jnp.stack(outs, axis=2).astype(p.dtype)
    y = jnp.einsum('bsgc,gcd->bsgd', pooled, w_pool).reshape(B, S, POOL_WIDTH)
    return y * pool_scale

def forgetting_attention(q, k, v, log_f):
    B, S, H, Dh = q.shape
    F = jnp.cumsum(log_f, axis=1).transpose(0, 2, 1)
    scale = Dh ** -0.5
    outs = []
    for i in range(S // Q_BLOCK):
        q0 = i * Q_BLOCK
        kv_len = q0 + Q_BLOCK
        s = jnp.einsum('bqhd,bkhd->bhqk', q[:, q0:kv_len], k[:, :kv_len]).astype(jnp.float32) * scale
        s = s + F[:, :, q0:kv_len, None] - F[:, :, None, :kv_len]
        qpos = q0 + jnp.arange(Q_BLOCK)
        kpos = jnp.arange(kv_len)
        s = jnp.where(kpos[None, :] <= qpos[:, None], s, -jnp.inf)
        pr = jax.nn.softmax(s, axis=-1)
        outs.append(jnp.einsum('bhqk,bkhd->bqhd', pr.astype(v.dtype), v[:, :kv_len]))
    return jnp.concatenate(outs, axis=1)

def peer_ffn(h, w_query, sub_keys, expert_u, expert_v):
    B, S, D = h.shape
    T = B * S
    ht = h.reshape(T, D)
    q = (ht @ w_query).reshape(T, PEER_HEADS, 2, PEER_QUERY // 2)
    s1 = jnp.einsum('thc,kc->thk', q[:, :, 0], sub_keys[0]).astype(jnp.float32)
    s2 = jnp.einsum('thc,kc->thk', q[:, :, 1], sub_keys[1]).astype(jnp.float32)
    v1, i1 = lax.top_k(s1, PEER_TOPK)
    v2, i2 = lax.top_k(s2, PEER_TOPK)
    cand_s = (v1[..., :, None] + v2[..., None, :]).reshape(T, PEER_HEADS, PEER_TOPK * PEER_TOPK)
    cand_i = (i1[..., :, None] * PEER_KEYS + i2[..., None, :]).reshape(T, PEER_HEADS, PEER_TOPK * PEER_TOPK)
    top_s, top_pos = lax.top_k(cand_s, PEER_TOPK)
    expert_idx = jnp.take_along_axis(cand_i, top_pos, axis=-1)
    gates = jax.nn.softmax(top_s, axis=-1).astype(h.dtype)

    nb = T // PEER_TOKEN_BLOCK

    def block(args):
        xb, idx, g = args
        u = expert_u[idx]
        a = jax.nn.gelu(jnp.einsum('thkd,td->thk', u, xb), approximate=False)
        return jnp.einsum('thk,thkd->td', g * a, expert_v[idx])

    y = lax.map(block, (ht.reshape(nb, PEER_TOKEN_BLOCK, D),
                        expert_idx.reshape(nb, PEER_TOKEN_BLOCK, PEER_HEADS, PEER_TOPK),
                        gates.reshape(nb, PEER_TOKEN_BLOCK, PEER_HEADS, PEER_TOPK)))
    return y.reshape(B, S, D)

def setup_inputs(seed: int = 0) -> dict:
    key = jax.random.key(seed)
    ks = jax.random.split(key, 16)
    f32 = jnp.float32
    nrm = lambda k, shape, s: jax.random.normal(k, shape, f32) * s
    return {
        "x": jax.random.normal(ks[0], (BATCH, SEQ, D_MODEL), f32),
        "norm1_g": 1.0 + nrm(ks[1], (DEPTH, D_MODEL), 0.02),
        "w_in": nrm(ks[2], (DEPTH, D_MODEL, IN_WIDTH), D_MODEL ** -0.5),
        "b_forget": jax.random.uniform(ks[3], (DEPTH, ATTN_HEADS), f32, 1.0, 4.0),
        "q_norm_g": 1.0 + nrm(ks[4], (DEPTH, ATTN_HEADS, HEAD_DIM), 0.02),
        "k_norm_g": 1.0 + nrm(ks[5], (DEPTH, ATTN_HEADS, HEAD_DIM), 0.02),
        "w_pool": nrm(ks[6], (DEPTH, len(POOL_WINDOWS), POOL_GROUP, POOL_GROUP), POOL_GROUP ** -0.5),
        "pool_scale": 1.0 + nrm(ks[7], (DEPTH, POOL_WIDTH), 0.02),
        "w_out": nrm(ks[8], (DEPTH, MIX_WIDTH, D_MODEL), MIX_WIDTH ** -0.5),
        "norm2_g": 1.0 + nrm(ks[9], (DEPTH, D_MODEL), 0.02),
        "w_query": nrm(ks[10], (DEPTH, D_MODEL, PEER_HEADS * PEER_QUERY), D_MODEL ** -0.5),
        "peer_sub_keys": nrm(ks[11], (DEPTH, 2, PEER_KEYS, PEER_QUERY // 2), (PEER_QUERY // 2) ** -0.5),
        "expert_u": nrm(ks[12], (DEPTH, PEER_EXPERTS, D_MODEL), D_MODEL ** -0.5),
        "expert_v": nrm(ks[13], (DEPTH, PEER_EXPERTS, D_MODEL), PEER_HEADS ** -0.5),
    }

def reference(x, norm1_g, w_in, b_forget, q_norm_g, k_norm_g, w_pool, pool_scale, w_out,
              norm2_g, w_query, peer_sub_keys, expert_u, expert_v):
    B, S, _ = x.shape
    for l in range(DEPTH):
        h = rms_norm(x, norm1_g[l])
        z = h @ w_in[l]
        o = POOL_WIDTH
        z_pool = z[..., :o]
        q = z[..., o:o + ATTN_WIDTH].reshape(B, S, ATTN_HEADS, HEAD_DIM)
        k = z[..., o + ATTN_WIDTH:o + 2 * ATTN_WIDTH].reshape(B, S, ATTN_HEADS, HEAD_DIM)
        v = z[..., o + 2 * ATTN_WIDTH:o + 3 * ATTN_WIDTH].reshape(B, S, ATTN_HEADS, HEAD_DIM)
        f_logit = z[..., o + 3 * ATTN_WIDTH:].astype(jnp.float32) + b_forget[l].astype(jnp.float32)
        log_f = jax.nn.log_sigmoid(f_logit)
        q = rms_norm(q, q_norm_g[l])
        k = rms_norm(k, k_norm_g[l])
        y_pool = pool_mixer(z_pool, w_pool[l], pool_scale[l])
        y_attn = forgetting_attention(q, k, v, log_f).reshape(B, S, ATTN_WIDTH)
        x = x + jnp.concatenate([y_pool, y_attn], axis=-1) @ w_out[l]
        x = x + peer_ffn(rms_norm(x, norm2_g[l]), w_query[l], peer_sub_keys[l], expert_u[l], expert_v[l])
    return x


_drawn_inputs = setup_inputs


def setup_inputs(seed=0):
    import zlib

    import numpy as np

    out = dict(_drawn_inputs(seed))
    spreads = {}
    factors = {'q_norm_g': 17.762, 'k_norm_g': 17.301, 'pool_scale': 8.341, 'norm2_g': 12.949}
    for name, (base, spread) in spreads.items():
        noise = np.random.default_rng([zlib.crc32(name.encode()), seed]).standard_normal(out[name].shape)
        drawn = base * np.exp(spread * noise) if base else spread * noise
        out[name] = __import__('jax').numpy.asarray(drawn.astype(out[name].dtype))
    for name, factor in factors.items():
        out[name] = (out[name] * factor).astype(out[name].dtype)
    return out
```

```python
import concourse.bass as bass
from concourse import mybir
from contextlib import ExitStack

F32 = mybir.dt.float32
F32R = mybir.dt.float32r
U32 = mybir.dt.uint32
ALU = mybir.AluOpType
ACT = mybir.ActivationFunctionType
AX = mybir.AxisListType

P = 128
T = 512
D = 1024
KD = D // P
TB = T // P
HEADS, DH = 8, 64
WINDOWS = (2, 4, 8, 16)
PH = 8
TOPK = 16
NKEY = 128
NCH = 128
PAD = 16
EPS = 1e-6
LOWEST = -3.0e38

V_W, Q_W = 1, 5
POOL_W, OUT_W, QUERY_W = 13, 17, 25
N_W = QUERY_W + 2 * PH
RAW, SPLIT = 4, 2

C_ID, C_MASK, C_IOTA, C_BLOCK, C_ONES, C_CNT, C_EPS = 0, 128, 640, 768, 896, 1024, 1088
N_CONST = 1092
G1, G2, QG, KG, PS, BF = 0, 8, 16, 20, 24, 28
N_VEC = 29


def program(nc, xT, wst, vecs, consts, w_pool, keysT, uT, v, out):
    g_dram = nc.dram_tensor("gates_dram", (NCH, P, T), F32, kind="Internal").ap()
    f_dram = nc.dram_tensor("forget_dram", (HEADS, T), F32, kind="Internal").ap()
    ctx = ExitStack()
    with ctx:
        def sb(name, shape, dt=F32, where=ctx):
            return where.enter_context(nc.sbuf_tensor(name, shape, dt))

        def sem(name):
            return ctx.enter_context(nc.semaphore(name))

        cst = sb("cst", [P, N_CONST])
        vec = sb("vec", [P, N_VEC])
        x = sb("x", [P, KD, T])
        hh = sb("hh", [P, KD, T], F32R)
        hl = sb("hl", [P, KD, T], F32R)
        raw = sb("raw", [P, RAW, D])
        wh = sb("wh", [P, SPLIT, D], F32R)
        wl = sb("wl", [P, SPLIT, D], F32R)
        root = sb("root", [P, T])
        var = sb("var", [P, T])
        rinv = sb("rinv", [P, T])
        newt = sb("newt", [P, T])

        mixers = ExitStack()
        mh = sb("mh", [P, KD, T], F32R, mixers)
        ml = sb("ml", [P, KD, T], F32R, mixers)
        qn = sb("qn", [P, 4, T], where=mixers)
        kn = sb("kn", [P, 4, T], where=mixers)
        vs = sb("vs", [P, TB, T], where=mixers)
        pr = sb("pr", [P, 2, TB, T], where=mixers)
        pT = sb("pT", [P, 2, 1280], where=mixers)
        nf = sb("nf", [P, 2, T], where=mixers)
        zc = sb("zc", [P, 2, T], where=mixers)
        sq = sb("sq", [P, 2, T], where=mixers)
        pad = sb("pad", [P, 3, PAD + T], where=mixers)
        pm = sb("pm", [P, T], where=mixers)
        fg = sb("fg", [HEADS, 3, T], where=mixers)
        rmax = sb("rmax", [P, 2, TB], where=mixers)
        nmax = sb("nmax", [P, 2, TB], where=mixers)
        rsum = sb("rsum", [P, 2, TB], where=mixers)
        rrec = sb("rrec", [P, 2, TB], where=mixers)
        wp = sb("wp", [P, 4, P], where=mixers)
        mixers.close()

        slotT = sb("slotT", [P, 3, T])
        retr = ExitStack()
        keys = sb("keys", [P, 2, NKEY], where=retr)
        qh = sb("qh", [P, 2, T], where=retr)
        sc = sb("sc", [P, 4, TB, NKEY], where=retr)
        sc2 = sb("sc2", [P, TB, NKEY], where=retr)
        kv = sb("kv", [P, 2, TB, TOPK], where=retr)
        ku = sb("ku", [P, 2, TB, TOPK], U32, where=retr)
        kf = sb("kf", [P, 2, TB, TOPK], where=retr)
        cand = sb("cand", [P, TB, TOPK, TOPK], where=retr)
        cand2 = sb("cand2", [P, TB, TOPK * TOPK], where=retr)
        tv = sb("tv", [P, TB, TOPK], where=retr)
        pos = sb("pos", [P, TB, TOPK], U32, where=retr)
        ab = sb("ab", [P, 2, TB, TOPK], U32, where=retr)
        abf = sb("abf", [P, 2, TB, TOPK], where=retr)
        hit = sb("hit", [P, 2, TB, TOPK, TOPK], where=retr)
        hit2 = sb("hit2", [P, 2, TB, TOPK, TOPK], where=retr)
        gd = sb("gd", [P, TB, TOPK], where=retr)
        ge = sb("ge", [P, TB, TOPK], where=retr)
        tick = sb("tick", [P, 1], where=retr)
        gs = sb("gs", [P, TB], where=retr)
        gr = sb("gr", [P, TB], where=retr)
        sel = sb("sel", [P, 3, TB, PH, TOPK], where=retr)
        retr.close()

        gate = ExitStack()
        gbuf = sb("gbuf", [P, NCH, P], where=gate)
        ohb = sb("ohb", [P, 2, 4, P], where=gate)
        oha = sb("oha", [P, 2, 4, P], where=gate)
        gate.close()

        exp = ExitStack()
        vraw = sb("vraw", [P, 2, D], where=exp)
        vh = sb("vh", [P, 4, D], F32R, exp)
        vl = sb("vl", [P, 4, D], F32R, exp)
        gt = sb("gt", [P, 2, T], where=exp)
        act_a = sb("act_a", [P, 2, T], where=exp)
        wf = sb("wf", [P, 2, T], where=exp)
        Wh = sb("Wh", [P, 4, T], F32R, exp)
        Wl = sb("Wl", [P, 4, T], F32R, exp)
        exp.close()

        bank = [ctx.enter_context(nc.psum_tensor(f"bank{i}", [P, T], F32)) for i in range(8)]
        SS, PV = 2, 3
        S_BANK, PT_BANK = 4, 6

        ident = cst[:, C_ID:C_ID + P]
        iota = cst[:, C_IOTA:C_IOTA + P]
        block_ones = cst[:, C_BLOCK:C_BLOCK + P]
        ones = cst[:, C_ONES:C_ONES + P]
        mask = cst[:, C_MASK + 3 * P:C_MASK + 4 * P]

        in_consts, in_x, in_keys = sem("in_consts"), sem("in_x"), sem("in_keys")
        raw_in = [sem(f"raw_in{i}") for i in range(RAW)]
        w_hi, w_lo, w_used = sem("w_hi"), sem("w_lo"), sem("w_used")
        sq_ready, sq_used = sem("sq_ready"), sem("sq_used")
        var_ready, root_ready = sem("var_ready"), sem("root_ready")
        h_ready, h_hi, h_lo = sem("h_ready"), sem("h_hi"), sem("h_lo")
        zc_ready, zc_used, v_saved = sem("zc_ready"), sem("zc_used"), sem("v_saved")
        f_taken, f_abs, f_ln, f_done, f_stored = (sem("f_taken"), sem("f_abs"), sem("f_ln"), sem("f_done"),
                                                  sem("f_stored"))
        nf_in = [sem("nf_in0"), sem("nf_in1")]
        s_ready, s_masked, e_ready, p_scaled = sem("s_ready"), sem("s_masked"), sem("e_ready"), sem("p_scaled")
        pt_ready, pt_saved, pv_ready = sem("pt_ready"), sem("pt_saved"), sem("pv_ready")
        att_hi, att_lo = sem("att_hi"), sem("att_lo")
        pool_prod, pool_hi, pool_lo, x1_ready = sem("pool_prod"), sem("pool_hi"), sem("pool_lo"), sem("x1_ready")
        qh_ready, sc_prod, sc_ready, sc_used = sem("qh_ready"), sem("sc_prod"), sem("sc_ready"), sem("sc_used")
        gd_ready, ge_ready, sel_ready = sem("gd_ready"), sem("ge_ready"), sem("sel_ready")
        tr_ready, tr_saved = sem("tr_ready"), sem("tr_saved")
        oh_ready, oh_used, gp_used, gp_stored = sem("oh_ready"), sem("oh_used"), sem("gp_used"), sem("gp_stored")
        gelu_done, w_ready, v_hi, v_lo = sem("gelu_done"), sem("w_ready"), sem("v_hi"), sem("v_lo")
        y_ready, y_added = sem("y_ready"), sem("y_added")
        vraw_in = [sem("vraw_in0"), sem("vraw_in1")]
        gt_in = [sem("gt_in0"), sem("gt_in1")]
        dve_done = sem("dve_done")
        stored = sem("stored")

        FREE_BANKS, FREE_SC, FREE_OH, FREE_Y = 2, 4, 2, KD

        qk = [("proj", Q_W + i) for i in range(8)]
        ss = [("ss", i) for i in range(8)]
        stages = [("norm1", 0), ("proj", 0)] + [("proj", V_W + i) for i in range(4)]
        stages += [qk[0], qk[1], ss[0], qk[2], ss[1], qk[3], ss[2], ("score", 0)]
        fill = [[qk[4], ss[3]], [qk[5], ss[4]], [qk[6], ss[5]], [qk[7], ss[6]], [ss[7], ("proj", POOL_W)],
                [("proj", POOL_W + 1), ("poolmix", 0)], [("proj", POOL_W + 2), ("poolmix", 1)],
                [("proj", POOL_W + 3), ("poolmix", 2)]]
        for h in range(HEADS):
            stages += [("score", h + 1)] * (h + 1 < HEADS) + fill[h] + [("attend", h)]
        stages += [("poolmix", 3)] + [("proj", OUT_W + m) for m in range(KD)] + [("norm2", 0)]

        def kind(n):
            return ("f" if n < V_W else "v" if n < Q_W else "qk" if n < POOL_W else "pool" if n < OUT_W else "out")

        def bank_of(n):
            return (n if n < V_W else n - 4) % 2

        def taken(n):
            return {"f": (f_taken, 1), "qk": (zc_ready, n - Q_W + 1), "pool": (zc_ready, n - Q_W + 1),
                    "out": (x1_ready, n - OUT_W + 1)}[kind(n)]

        SQ_QK, SQ_OUT = KD, 2 * KD
        PT_AT = ((0, 512), (512, 384), (896, 384))
        KEY_AT = (0, 512, 896, 1152)

        block = ctx.enter_context(nc.Block())

        @block.sync
        def _(sp):
            sp.dma_start(x[:, :, :], xT).then_inc(in_x, 16)
            sp.dma_start(cst[:, :], consts).then_inc(in_consts, 16)
            sp.dma_start(vec[:, :], vecs).then_inc(in_consts, 16)
            sp.dma_start(wp[:, :, :], w_pool).then_inc(in_consts, 16)

            for n in range(QUERY_W):
                if n == 9:
                    sp.wait_ge(f_done, 1)
                    sp.dma_start(f_dram, fg[:, 2, :]).then_inc(f_stored, 16)
                    sp.wait_ge(f_stored, 16)
                if 9 <= n < 9 + HEADS:
                    h = n - 9
                    if h >= 2:
                        sp.wait_ge(s_masked, TB * (h - 1))
                    sp.dma_start(nf[:, h % 2, :], f_dram[h:h + 1, :].broadcast_to([P, T])).then_inc(nf_in[h % 2], 16)
                if n >= RAW:
                    sp.wait_ge(w_lo, n - RAW + 1)
                sp.dma_start(raw[:, n % RAW, :], wst[n]).then_inc(raw_in[n % RAW], 16)

            sp.wait_ge(h_lo, 2 * KD)
            sp.dma_start(keys[:, :, :], keysT).then_inc(in_keys, 16)
            with sp.Fori(0, PH // 2) as it:
                for k in range(4):
                    slot = (QUERY_W + k) % RAW
                    sp.wait_ge(w_lo, it * 4 + (QUERY_W + k - RAW + 1))
                    sp.dma_start(raw[:, slot, :], wst[bass.ds(it * 4 + (QUERY_W + k), 1)]
                                 .rearrange("a p n -> p (a n)")).then_inc(raw_in[slot], 16)

            def load_u(it, k):
                slot = (N_W + k) % RAW
                sp.wait_ge(w_lo, it * 4 + (N_W + k - RAW + 1))
                sp.dma_start(raw[:, slot, :], uT[bass.ds(it * 4 + k, 1)].rearrange("a p n -> p (a n)"))\
                  .then_inc(raw_in[slot], 16)

            def load_vg(it, k, first=False):
                if not first:
                    sp.wait_ge(v_lo, it * 4 + (k - 1))
                sp.dma_start(vraw[:, k % 2, :], v[bass.ds(it * 4 + k, 1)].rearrange("a p n -> p (a n)"))\
                  .then_inc(vraw_in[k % 2], 16)
                if not first:
                    sp.wait_ge(w_ready, it * 4 + (k - 1))
                sp.dma_start(gt[:, k % 2, :], g_dram[bass.ds(it * 4 + k, 1)].rearrange("a p n -> p (a n)"))\
                  .then_inc(gt_in[k % 2], 16)

            load_u(0, 0)
            load_u(0, 1)
            for b in range(TB):
                sp.wait_ge(gp_used, FREE_BANKS + 32 * (b + 1))
                sp.dma_start(g_dram[:, :, b * P:(b + 1) * P].rearrange("i j t -> j i t"), gbuf[:, :, :])\
                  .then_inc(gp_stored, 16)
            sp.wait_ge(gp_stored, 16 * TB)
            load_vg(0, 0, True)
            load_vg(0, 1, True)
            with sp.Fori(0, NCH // 4 - 1) as it:
                for k in range(2, 6):
                    load_u(it, k)
                    load_vg(it, k)
            for k in (2, 3):
                load_u(NCH // 4 - 1, k)
                load_vg(NCH // 4 - 1, k)
            sp.wait_ge(y_added, FREE_Y + KD * (NCH // 2))
            sp.dma_start(out, x[:, :, :]).then_inc(stored, 16)
            sp.wait_ge(stored, 16)

        @block.gpsimd
        def _(pool):
            def split_lo(n, slot_raw, slot):
                pool.wait_ge(w_hi, n + 1)
                pool.tensor_tensor(wl[:, slot, :], raw[:, slot_raw, :], wh[:, slot, :].bitcast(F32), ALU.subtract)\
                    .then_inc(w_lo, 1)

            def split_v(it, k):
                pool.wait_ge(v_hi, it * 4 + (k + 1))
                pool.tensor_tensor(vl[:, k % 4, :], vraw[:, k % 2, :], vh[:, k % 4, :].bitcast(F32), ALU.subtract)\
                    .then_inc(v_lo, 1)

            for n in range(QUERY_W):
                split_lo(n, n % RAW, n % SPLIT)
            with pool.Fori(0, PH // 2) as it:
                for k in range(4):
                    split_lo(it * 4 + (QUERY_W + k), (QUERY_W + k) % RAW, (QUERY_W + k) % SPLIT)
            for k in (0, 1):
                split_lo(N_W + k, (N_W + k) % RAW, (N_W + k) % SPLIT)

            def chunk(it, k, last=False):
                split_v(it, k)
                if not last:
                    split_lo(it * 4 + (N_W + k + 2), (N_W + k + 2) % RAW, (N_W + k) % SPLIT)

            chunk(0, 0)
            chunk(0, 1)
            with pool.Fori(0, NCH // 4 - 1) as it:
                for k in range(2, 6):
                    chunk(it, k)
            chunk(NCH // 4 - 1, 2, True)
            chunk(NCH // 4 - 1, 3, True)

        @block.scalar
        def _(act):
            def split_hi(n, static, round_):
                act.wait_ge(raw_in[static % RAW], round_ * 16)
                if static >= SPLIT:
                    act.wait_ge(w_used, n - (SPLIT - 1))
                act.activation(wh[:, static % SPLIT, :], raw[:, static % RAW, :], ACT.Copy).then_inc(w_hi, 1)

            def square(i, src):
                if i >= 2:
                    act.wait_ge(sq_used, i - 1)
                act.activation(sq[:, i % 2, :], src, ACT.Square).then_inc(sq_ready, 1)

            act.wait_ge(in_consts, 48)
            act.wait_ge(in_x, 16)
            split_hi(0, 0, 1)
            split_hi(1, 1, 1)
            roots = 0
            for what, i in stages:
                if what == "norm1":
                    for k in range(KD):
                        square(k, x[:, k, :])
                elif what == "proj":
                    n = i
                    if kind(n) == "f":
                        act.wait_ge(f_abs, 1)
                        act.activation(fg[:, 1, :], fg[:, 1, :], ACT.Exp).then_inc(f_ln, 1)
                        act.wait_ge(f_ln, 1)
                        act.activation(fg[:, 1, :], fg[:, 1, :], ACT.Ln, bias=cst[0:HEADS, C_EPS:C_EPS + 1])\
                           .then_inc(f_ln, 1)
                    elif kind(n) in ("qk", "pool"):
                        z = n - Q_W
                        act.wait_ge(w_used, n + 1)
                        if z >= 2:
                            act.wait_ge(zc_used, z - 1)
                        else:
                            act.wait_ge(h_lo, KD)
                        act.activation(zc[:, z % 2, :], bank[bank_of(n)][:, :], ACT.Copy).then_inc(zc_ready, 1)
                        if kind(n) == "qk":
                            act.wait_ge(zc_ready, z + 1)
                            square(SQ_QK + z, zc[:, z % 2, :])
                    elif kind(n) == "out":
                        act.wait_ge(x1_ready, n - OUT_W + 1)
                        square(SQ_OUT + n - OUT_W, x[:, n - OUT_W, :])
                    if n + 2 < QUERY_W:
                        split_hi(n + 2, n + 2, (n + 2) // RAW + 1)
                elif what == "poolmix":
                    act.wait_ge(pool_prod, i + 1)
                    act.activation(mh[:, i, :], bank[SS][:, :], ACT.Copy, scale=vec[:, PS + i:PS + i + 1])\
                       .then_inc(pool_hi, 1)
                elif what == "score":
                    for b in range(TB):
                        act.wait_ge(s_masked, TB * i + b + 1)
                        act.activation(pr[:, i % 2, b, 0:(b + 1) * P], pr[:, i % 2, b, 0:(b + 1) * P], ACT.Exp,
                                       bias=nmax[:, i % 2, b:b + 1], accum_out=rsum[:, i % 2, b:b + 1])\
                           .then_inc(e_ready, 1)
                elif what == "attend":
                    for g, (at, size) in enumerate(PT_AT):
                        act.wait_ge(pt_ready, 3 * i + g + 1)
                        if i >= 2:
                            act.wait_ge(pv_ready, i - 1)
                        act.activation(pT[:, i % 2, at:at + size], bank[PT_BANK + (3 * i + g) % 2][:, 0:size],
                                       ACT.Copy).then_inc(pt_saved, 1)
                    rows = slice(DH * (i % 2), DH * (i % 2) + DH)
                    act.wait_ge(pv_ready, i + 1)
                    act.activation(mh[rows, 4 + i // 2, :], bank[PV][rows, :], ACT.Copy).then_inc(att_hi, 1)
                if what in ("norm1", "ss", "norm2"):
                    act.wait_ge(var_ready, roots + 1)
                    act.activation(root[:, :], var[:, :], ACT.Sqrt).then_inc(root_ready, 1)
                    roots += 1
                if what in ("norm1", "norm2"):
                    base = 0 if what == "norm1" else KD
                    for k in range(KD):
                        act.wait_ge(h_ready, base + k + 1)
                        act.activation(hh[:, k, :], zc[:, k % 2, :], ACT.Copy).then_inc(h_hi, 1)
                if what == "norm2":
                    for n in (QUERY_W, QUERY_W + 1):
                        split_hi(n, n, n // RAW + 1)

            act.sem_inc(qh_ready, FREE_BANKS)
            act.sem_inc(sc_ready, FREE_BANKS)
            with act.Fori(0, PH // 2) as it:
                for k in range(4):
                    act.wait_ge(w_used, it * 4 + (QUERY_W + k + 1))
                    act.activation(qh[:, k % 2, :], bank[bank_of(QUERY_W + k)][:, :], ACT.Copy).then_inc(qh_ready, 1)
                    s2 = QUERY_W + k + 2
                    split_hi(it * 4 + s2, s2, it + (s2 // RAW + 1))
                    act.wait_ge(sc_prod, it * 4 + (k + 1))
                    act.wait_ge(sc_used, it * 4 + (k + 1))
                    act.activation(sc[:, k, :, :].rearrange("p b k -> p (b k)"), bank[S_BANK + k % 2][:, :], ACT.Copy)\
                       .then_inc(sc_ready, 1)
                    if k % 2:
                        act.wait_ge(gd_ready, it * 2 + (k // 2 + 1))
                        act.activation(ge[:, :, :], gd[:, :, :], ACT.Exp).then_inc(ge_ready, 1)
            for a in range(3):
                act.wait_ge(tr_ready, a + 1)
                act.activation(slotT[:, a, :], bank[PT_BANK + a % 2][:, :], ACT.Copy).then_inc(tr_saved, 1)

            act.sem_inc(gp_used, FREE_BANKS)
            for b in range(TB):
                if b >= 1:
                    act.wait_ge(gp_stored, 16 * b)
                with act.Fori(0, P // 8) as it:
                    for k in range(2):
                        act.wait_ge(oh_used, it * 2 + (FREE_OH + 32 * b + k + 1))
                        act.activation(gbuf[:, :, bass.ds(it * 8 + 4 * k, 4)],
                                       bank[k][:, :].rearrange("j (t i) -> j i t", t=4), ACT.Copy).then_inc(gp_used, 1)

            def chunk(it, k, first=False, last=False):
                act.wait_ge(vraw_in[k % 2], it * 32 + 16 * (k // 2 + 1))
                if not first:
                    act.wait_ge(y_ready, it * 16 + KD * (k // 2))
                act.activation(vh[:, k % 4, :], vraw[:, k % 2, :], ACT.Copy).then_inc(v_hi, 1)
                act.wait_ge(w_used, it * 4 + (N_W + k + 1))
                if not first:
                    act.wait_ge(w_ready, it * 4 + (k - 1))
                act.activation(act_a[:, k % 2, :], bank[k % 2][:, :], ACT.Gelu).then_inc(gelu_done, 1)
                if not last:
                    s2 = N_W + k + 2
                    split_hi(it * 4 + s2, s2, it + (s2 // RAW + 1))

            chunk(0, 0, first=True)
            chunk(0, 1, first=True)
            with act.Fori(0, NCH // 4 - 1) as it:
                for k in range(2, 6):
                    chunk(it, k)
            for k in (2, 3):
                chunk(NCH // 4 - 1, k, last=True)

        @block.tensor
        def _(pe):
            def three(dst, ah, al, bh, bl, start, stop):
                pe.matmul(dst, ah, bh, start=start, stop=False)
                pe.matmul(dst, ah, bl, start=False, stop=False)
                return pe.matmul(dst, al, bh, start=False, stop=stop)

            def project(dst, s, right_h, right_l):
                for k in range(KD):
                    last = three(dst, wh[:, s, k * P:(k + 1) * P], wl[:, s, k * P:(k + 1) * P],
                                 right_h[:, k, :], right_l[:, k, :], k == 0, k == KD - 1)
                last.then_inc(w_used, 1)

            def sum_square(i, weights, start, stop):
                pe.wait_ge(sq_ready, i + 1)
                pe.matmul(bank[SS][:, :], weights, sq[:, i % 2, :], start=start, stop=stop).then_inc(sq_used, 1)

            pe.wait_ge(in_consts, 48)
            last_in_bank = {}
            for what, i in stages:
                if what == "norm1":
                    for k in range(KD):
                        sum_square(k, ones, k == 0, k == KD - 1)
                elif what == "proj":
                    n, kd = i, kind(i)
                    pe.wait_ge(w_lo, n + 1)
                    if n == 0:
                        pe.wait_ge(h_lo, KD)
                    if kd == "v":
                        for b in range(TB):
                            for kk in range(2):
                                k = 2 * (n - V_W) + kk
                                at, w = slice(b * P, (b + 1) * P), slice(kk * T, (kk + 1) * T)
                                last = three(bank[S_BANK + b][:, :], hh[:, k, at], hl[:, k, at],
                                             wh[:, n % SPLIT, w], wl[:, n % SPLIT, w], k == 0, k == KD - 1)
                        last.then_inc(w_used, 1)
                        continue
                    if bank_of(n) in last_in_bank:
                        pe.wait_ge(*taken(last_in_bank[bank_of(n)]))
                    last_in_bank[bank_of(n)] = n
                    if n == OUT_W:
                        pe.wait_ge(att_lo, HEADS)
                        pe.wait_ge(pool_lo, 4)
                    project(bank[bank_of(n)][:, :], n % SPLIT, *((mh, ml) if kd == "out" else (hh, hl)))
                    if n > OUT_W:
                        sum_square(SQ_OUT + n - OUT_W - 1, ones, n == OUT_W + 1, False)
                elif what == "ss":
                    pe.wait_ge(var_ready, 1 + i)
                    sum_square(SQ_QK + i, block_ones, True, True)
                elif what == "poolmix":
                    pe.wait_ge(zc_used, 9 + i)
                    if i:
                        pe.wait_ge(pool_lo, i)
                    else:
                        pe.wait_ge(var_ready, 9)
                    pe.matmul(bank[SS][:, :], wp[:, i, :], pm[:, :], start=True, stop=True).then_inc(pool_prod, 1)
                elif what == "score":
                    h, c = i, i // 2
                    rows = slice(DH * (h % 2), DH * (h % 2) + DH)
                    pe.wait_ge(zc_used, 2 * c + 2)
                    for b in range(TB):
                        n = TB * h + b
                        if n >= 2:
                            pe.wait_ge(s_masked, n - 1)
                        else:
                            pe.wait_ge(v_saved, TB)
                        pe.matmul(bank[S_BANK + n % 2][:, 0:(b + 1) * P], qn[rows, c, b * P:(b + 1) * P],
                                  kn[rows, c, 0:(b + 1) * P], start=True, stop=True).then_inc(s_ready, 1)
                elif what == "attend":
                    h = i
                    pe.wait_ge(p_scaled, TB * (h + 1))
                    for g, pieces in enumerate(([(0, b) for b in range(4)], [(1, b) for b in range(1, 4)],
                                                [(2, 2), (2, 3), (3, 3)])):
                        n = 3 * h + g
                        if n >= 2:
                            pe.wait_ge(pt_saved, n - 1)
                        for at, (key, b) in enumerate(pieces):
                            last = pe.transpose(bank[PT_BANK + n % 2][:, at * P:(at + 1) * P],
                                                pr[:, h % 2, b, key * P:(key + 1) * P], ident)
                        last.then_inc(pt_ready, 1)
                    pe.wait_ge(pt_saved, 3 * h + 3)
                    if h:
                        pe.wait_ge(att_lo, h)
                    for key in range(TB):
                        size = (TB - key) * P
                        last = pe.matmul(bank[PV][:, key * P:T], vs[:, key, (h // 2) * P:(h // 2 + 1) * P],
                                         pT[:, h % 2, KEY_AT[key]:KEY_AT[key] + size],
                                         start=(key == 0), stop=(key == TB - 1))
                    last.then_inc(pv_ready, 1)
                elif what == "norm2":
                    sum_square(SQ_OUT + KD - 1, ones, False, True)

            pe.wait_ge(h_lo, 2 * KD)
            pe.wait_ge(in_keys, 16)

            def scores(it, k):
                pe.wait_ge(qh_ready, it * 4 + (FREE_BANKS + k + 1))
                pe.wait_ge(sc_ready, it * 4 + (k + 1))
                for b in range(TB):
                    last = pe.matmul(bank[S_BANK + k % 2][:, b * P:(b + 1) * P], qh[:, k % 2, b * P:(b + 1) * P],
                                     keys[:, k % 2, :], start=True, stop=True)
                last.then_inc(sc_prod, 1)

            with pe.Fori(0, PH // 2) as it:
                for k in range(4):
                    pe.wait_ge(w_lo, it * 4 + (QUERY_W + k + 1))
                    pe.wait_ge(qh_ready, it * 4 + (k + 1))
                    project(bank[bank_of(QUERY_W + k)][:, :], (QUERY_W + k) % SPLIT, hh, hl)
                    if k:
                        scores(it, k - 1)
                scores(it, 3)

            pe.wait_ge(sel_ready, 1)
            for a in range(3):
                if a == 2:
                    pe.wait_ge(tr_saved, 1)
                for b in range(TB):
                    last = pe.transpose(bank[PT_BANK + a % 2][:, b * P:(b + 1) * P],
                                        sel[:, a, b, :, :].rearrange("p h k -> p (h k)"), ident)
                last.then_inc(tr_ready, 1)

            pe.sem_inc(oh_used, FREE_OH)
            with pe.Fori(0, T // 8) as it:
                for k in range(2):
                    pe.wait_ge(oh_ready, it * 2 + (k + 1))
                    pe.wait_ge(gp_used, it * 2 + (k + 1))
                    for t in range(4):
                        last = pe.matmul(bank[k][:, t * P:(t + 1) * P], ohb[:, k, t, :], oha[:, k, t, :],
                                         start=True, stop=True)
                    last.then_inc(oh_used, 1)

            pe.sem_inc(y_ready, FREE_Y)

            def up(it, k, first=False):
                pe.wait_ge(w_lo, it * 4 + (N_W + k + 1))
                if first:
                    pe.wait_ge(gp_used, FREE_BANKS + T // 4)
                else:
                    pe.wait_ge(gelu_done, it * 4 + (k - 1))
                project(bank[k % 2][:, :], (N_W + k) % SPLIT, hh, hl)

            def down(it, g):
                pe.wait_ge(w_ready, it * 4 + (2 * g + 2))
                pe.wait_ge(v_lo, it * 4 + (2 * g + 2))
                for m in range(KD):
                    pe.wait_ge(y_added, it * 16 + (KD * g + m - 3 + FREE_Y))
                    for j in range(2):
                        s, at = 2 * g + j, slice(m * P, (m + 1) * P)
                        last = three(bank[4 + m % 4][:, :], vh[:, s, at], vl[:, s, at],
                                     Wh[:, s, :], Wl[:, s, :], j == 0, j == 1)
                    last.then_inc(y_ready, 1)

            up(0, 0, True)
            up(0, 1, True)
            with pe.Fori(0, NCH // 4 - 1) as it:
                up(it, 2)
                up(it, 3)
                down(it, 0)
                up(it, 4)
                up(it, 5)
                down(it, 1)
            up(NCH // 4 - 1, 2)
            up(NCH // 4 - 1, 3)
            down(NCH // 4 - 1, 0)
            down(NCH // 4 - 1, 1)

        @block.vector
        def _(dve):
            base, count = 0, 0

            def lo_part(dve, i, k):
                dve.wait_ge(h_hi, i + 1)
                dve.tensor_tensor(hl[:, k, :], zc[:, k % 2, :], hh[:, k, :].bitcast(F32), ALU.subtract)\
                   .then_inc(h_lo, 1)

            def step(instruction):
                nonlocal count
                count += 1
                instruction.then_inc(dve_done, 1)

            def fence():
                dve.wait_ge(dve_done, base + count)

            def fence_apart():
                dve.drain()

            for i in range(3):
                step(dve.memset(pad[:, i, 0:PAD], 0.0))
            dve.wait_ge(in_consts, 48)
            dve.wait_ge(in_x, 16)
            roots = 0
            for what, i in stages:
                if what in ("norm1", "ss", "norm2"):
                    scale, eps = {"norm1": (1.0 / D, EPS), "norm2": (1.0 / D, EPS),
                                  "ss": (1.0, DH * EPS) if i % 2 == 0 else (1.0 / DH, EPS)}[what]
                    dve.wait_ge(sq_used, {"norm1": KD, "ss": SQ_QK + i + 1, "norm2": 3 * KD}[what])
                    fence()
                    dve.tensor_scalar(var[:, :], bank[SS][:, :], scale, eps, ALU.mult, ALU.add).then_inc(var_ready, 1)
                    dve.wait_ge(root_ready, roots + 1)
                    roots += 1
                    step(dve.reciprocal(rinv[:, :], root[:, :]))
                    fence()
                    step(dve.tensor_tensor(newt[:, :], rinv[:, :], rinv[:, :], ALU.mult))
                    fence()
                    step(dve.tensor_tensor(newt[:, :], newt[:, :], var[:, :], ALU.mult))
                    fence()
                    step(dve.tensor_scalar(newt[:, :], newt[:, :], -0.5, 1.5, ALU.mult, ALU.add))
                    fence()
                    step(dve.tensor_tensor(rinv[:, :], newt[:, :], rinv[:, :], ALU.mult))
                    fence()
                if what == "ss":
                    n, c = i, i // 2
                    dst, g = (qn, QG) if i % 2 == 0 else (kn, KG)
                    dve.scalar_tensor_tensor(dst[:, c, :], zc[:, n % 2, :], vec[:, g + c:g + c + 1], rinv[:, :],
                                             ALU.mult, ALU.mult).then_inc(zc_used, 1)
                    dve.wait_ge(zc_used, i + 1)
                elif what in ("norm1", "norm2"):
                    first, g = (0, G1) if what == "norm1" else (KD, G2)
                    for k in range(KD):
                        if first + k >= 2 and k >= 2:
                            dve.wait_ge(h_lo, first + k - 1)
                        dve.scalar_tensor_tensor(zc[:, k % 2, :], x[:, k, :], vec[:, g + k:g + k + 1], rinv[:, :],
                                                 ALU.mult, ALU.mult).then_inc(h_ready, 1)
                        if k:
                            lo_part(dve, first + k - 1, k - 1)
                    lo_part(dve, first + KD - 1, KD - 1)
                elif what == "proj":
                    n, kd = i, kind(i)
                    if kd == "f":
                        dve.wait_ge(w_used, 1)
                        dve.tensor_scalar(fg[:, 0, :], bank[bank_of(n)][0:HEADS, :], vec[0:HEADS, BF:BF + 1], None,
                                          ALU.add).then_inc(f_taken, 1)
                        dve.wait_ge(f_taken, 1)
                        dve.scalar_tensor_tensor(fg[:, 1, :], fg[:, 0, :], -1.0, fg[:, 0, :], ALU.mult, ALU.min)\
                           .then_inc(f_abs, 1)
                        dve.wait_ge(f_ln, 2)
                        step(dve.scalar_tensor_tensor(fg[:, 0, :], fg[:, 0, :], 0.0, fg[:, 1, :],
                                                      ALU.min, ALU.subtract))
                        fence()
                        step(dve.tensor_scalar(fg[:, 0, :], fg[:, 0, :], -1.0, None, ALU.mult))
                        fence()
                        dve.tensor_tensor_scan(fg[:, 2, :], fg[:, 0, :], fg[:, 1, :], 0.0, ALU.add, ALU.bypass)\
                           .then_inc(f_done, 1)
                    elif n == Q_W - 1:
                        dve.wait_ge(w_used, Q_W)
                        for b in range(TB):
                            dve.tensor_copy(vs[:, b, :], bank[S_BANK + b][:, :]).then_inc(v_saved, 1)
                    elif kd == "pool":
                        g, z = n - POOL_W, n - Q_W
                        w = WINDOWS[g]
                        dve.wait_ge(zc_ready, z + 1)
                        fence()
                        step(dve.tensor_copy(pad[:, 0, PAD:], zc[:, z % 2, :]))
                        src, s = 0, 1
                        while s < w:
                            fence()
                            dst = 2 if src == 1 else 1
                            step(dve.tensor_tensor(pad[:, dst, PAD:], pad[:, src, PAD:],
                                                   pad[:, src, PAD - s:PAD + T - s], ALU.add))
                            src, s = dst, 2 * s
                        fence()
                        if g:
                            dve.wait_ge(pool_prod, g)
                        step(dve.scalar_tensor_tensor(pm[:, :], pad[:, src, PAD:], 1.0 / w, zc[:, z % 2, :],
                                                      ALU.mult, ALU.subtract))
                        fence()
                        step(dve.tensor_tensor(pm[:, 0:PAD], pad[:, src, PAD:2 * PAD],
                                               cst[:, C_CNT + PAD * g:C_CNT + PAD * (g + 1)], ALU.mult))
                        fence()
                        dve.tensor_tensor(pm[:, 0:PAD], pm[:, 0:PAD], zc[:, z % 2, 0:PAD], ALU.subtract)\
                           .then_inc(zc_used, 1)
                    elif kd == "out":
                        m = n - OUT_W
                        dve.wait_ge(w_used, n + 1)
                        dve.tensor_tensor(x[:, m, :], x[:, m, :], bank[bank_of(n)][:, :], ALU.add)\
                           .then_inc(x1_ready, 1)
                        if m == KD - 1:
                            dve.wait_ge(x1_ready, KD)
                elif what == "poolmix":
                    dve.wait_ge(pool_hi, i + 1)
                    dve.scalar_tensor_tensor(ml[:, i, :], bank[SS][:, :], vec[:, PS + i:PS + i + 1],
                                             mh[:, i, :].bitcast(F32), ALU.mult, ALU.subtract).then_inc(pool_lo, 1)
                elif what == "score":
                    h = i
                    dve.wait_ge(nf_in[h % 2], 16 * (h // 2 + 1))
                    if h >= 2:
                        dve.wait_ge(pt_ready, 3 * (h - 1))
                    for b in range(TB):
                        s = bank[S_BANK + (TB * h + b) % 2]
                        size = (b + 1) * P
                        dve.wait_ge(s_ready, TB * h + b + 1)
                        step(dve.tensor_tensor(s[:, b * P:size], s[:, b * P:size], mask, ALU.add))
                        fence()
                        step(dve.tensor_tensor_reduce(pr[:, h % 2, b, 0:size], s[:, 0:size], nf[:, h % 2, 0:size],
                                                      1.0, LOWEST, ALU.add, ALU.max, rmax[:, h % 2, b:b + 1]))
                        fence()
                        dve.tensor_scalar(nmax[:, h % 2, b:b + 1], rmax[:, h % 2, b:b + 1], -1.0, None, ALU.mult)\
                           .then_inc(s_masked, 1)
                    dve.wait_ge(e_ready, TB * (h + 1))
                    step(dve.reciprocal(rrec[:, h % 2, :], rsum[:, h % 2, :]))
                    fence()
                    for b in range(TB):
                        size = (b + 1) * P
                        dve.tensor_scalar(pr[:, h % 2, b, 0:size], pr[:, h % 2, b, 0:size], rrec[:, h % 2, b:b + 1],
                                          None, ALU.mult).then_inc(p_scaled, 1)
                elif what == "attend":
                    rows = slice(DH * (i % 2), DH * (i % 2) + DH)
                    dve.wait_ge(att_hi, i + 1)
                    dve.tensor_tensor(ml[rows, 4 + i // 2, :], bank[PV][rows, :],
                                      mh[rows, 4 + i // 2, :].bitcast(F32), ALU.subtract).then_inc(att_lo, 1)

            dve.sem_inc(sc_used, FREE_SC)
            fence()
            before = count
            with dve.Fori(0, PH // 2) as it:
                base, count = it * RETRIEVE_STEPS + before, 0
                for k in range(4):
                    half = k % 2
                    kt, ku_ = kv[:, half], ku[:, half]
                    s = sc[:, k]
                    dve.wait_ge(sc_ready, it * 4 + (FREE_BANKS + k + 1))
                    dve.memset(tick[:, :], 0.0)
                    fence_apart()
                    for b in range(TB):
                        step(dve.max(kt[:, b, 0:8], s[:, b, :]))
                    fence_apart()
                    for b in range(TB):
                        step(dve.max_index(ku_[:, b, 0:8], kt[:, b, 0:8], s[:, b, :]))
                        step(dve.match_replace(sc2[:, b, :], kt[:, b, 0:8], s[:, b, :], LOWEST))
                    fence_apart()
                    for b in range(TB):
                        ins = dve.max(kt[:, b, 8:16], sc2[:, b, :])
                        step(ins)
                    fence_apart()
                    for b in range(TB):
                        ins = dve.max_index(ku_[:, b, 8:16], kt[:, b, 8:16], sc2[:, b, :])
                        if b < TB - 1:
                            step(ins)
                        else:
                            ins.then_inc(sc_used, 1)
                    if half == 0:
                        continue
                    h = it * 2 + k // 2
                    dve.wait_ge(sc_used, it * 4 + (FREE_SC + k + 1))
                    wide = [P, TB, TOPK, TOPK]
                    step(dve.tensor_tensor(cand[:, :, :, :], kv[:, 0].unsqueeze(3).broadcast_to(wide),
                                           kv[:, 1].unsqueeze(2).broadcast_to(wide), ALU.add))
                    step(dve.tensor_copy(kf[:, :, :, :], ku[:, :, :, :]))
                    fence_apart()
                    flat = cand[:, :, :, :].rearrange("p b i j -> p b (i j)")
                    for b in range(TB):
                        step(dve.max(tv[:, b, 0:8], flat[:, b, :]))
                    fence_apart()
                    for b in range(TB):
                        step(dve.max_index(pos[:, b, 0:8], tv[:, b, 0:8], flat[:, b, :]))
                        step(dve.match_replace(cand2[:, b, :], tv[:, b, 0:8], flat[:, b, :], LOWEST))
                    fence_apart()
                    for b in range(TB):
                        step(dve.max(tv[:, b, 8:16], cand2[:, b, :]))
                    fence()
                    dve.tensor_tensor(gd[:, :, :], tv[:, :, :], tv[:, :, 0:1].broadcast_to([P, TB, TOPK]),
                                      ALU.subtract).then_inc(gd_ready, 1)
                    for b in range(TB):
                        step(dve.max_index(pos[:, b, 8:16], tv[:, b, 8:16], cand2[:, b, :]))
                    fence()
                    step(dve.tensor_scalar(ab[:, 0], pos[:, :, :], 4, None, ALU.logical_shift_right))
                    step(dve.tensor_scalar(ab[:, 1], pos[:, :, :], 15, None, ALU.bitwise_and))
                    fence()
                    step(dve.tensor_copy(abf[:, :, :, :], ab[:, :, :, :]))
                    fence()
                    for a in range(2):
                        step(dve.tensor_tensor(hit[:, a], abf[:, a].unsqueeze(3).broadcast_to(wide),
                                               iota[:, 0:TOPK].unsqueeze(1).unsqueeze(1).broadcast_to(wide),
                                               ALU.is_equal))
                    fence()
                    for a in range(2):
                        step(dve.tensor_tensor(hit2[:, a], hit[:, a], kf[:, a].unsqueeze(2).broadcast_to(wide),
                                               ALU.mult))
                    fence()
                    dve.wait_ge(ge_ready, it * 2 + (k // 2 + 1))
                    step(dve.tensor_reduce(gs[:, :], ge[:, :, :], AX.X, ALU.add))
                    for a in range(2):
                        step(dve.tensor_reduce(sel[:, a, :, bass.ds(h, 1), :].rearrange("p b a k -> p b (a k)"),
                                               hit2[:, a], AX.X, ALU.add))
                    fence()
                    step(dve.reciprocal(gr[:, :], gs[:, :]))
                    fence()
                    step(dve.tensor_tensor(sel[:, 2, :, bass.ds(h, 1), :].rearrange("p b a k -> p b (a k)"),
                                           ge[:, :, :], gr[:, :].unsqueeze(2).broadcast_to([P, TB, TOPK]), ALU.mult))
                assert count == RETRIEVE_STEPS, count
            base, count = 0, before + RETRIEVE_STEPS * (PH // 2)
            fence()
            dve.sem_inc(sel_ready, 1)

            dve.wait_ge(tr_saved, 3)
            with dve.Fori(0, T // 8) as it:
                for k in range(2):
                    dve.wait_ge(oh_used, it * 2 + (k + 1))
                    at = bass.ds(it * 8 + 4 * k, 4)
                    dve.tensor_tensor(ohb[:, k], iota.unsqueeze(1).broadcast_to([P, 4, P]),
                                      slotT[:, 1, at].unsqueeze(2).broadcast_to([P, 4, P]), ALU.is_equal)
                    for t in range(4):
                        one = bass.ds(it * 8 + (4 * k + t), 1)
                        last = dve.tensor_scalar(oha[:, k, t, :], iota, slotT[:, 0, one], slotT[:, 2, one],
                                                 ALU.is_equal, ALU.mult)
                    last.then_inc(oh_ready, 1)

            dve.sem_inc(y_added, FREE_Y)
            before = count
            base = before

            def weigh(it, k, first=False):
                nonlocal count
                slot = k % 4
                dve.wait_ge(gelu_done, it * 4 + (k + 1))
                dve.wait_ge(gt_in[k % 2], it * 32 + 16 * (k // 2 + 1))
                if not first:
                    dve.wait_ge(w_ready, it * 4 + (k - 1))
                base_ = it * 8 + (before + 2 * k)
                dve.tensor_tensor(wf[:, k % 2, :], gt[:, k % 2, :], act_a[:, k % 2, :], ALU.mult)\
                   .then_inc(dve_done, 1)
                dve.wait_ge(dve_done, base_ + 1)
                if not first:
                    dve.wait_ge(y_ready, it * 16 + KD * (k // 2))
                dve.tensor_copy(Wh[:, slot, :], wf[:, k % 2, :]).then_inc(dve_done, 1)
                dve.wait_ge(dve_done, base_ + 2)
                dve.tensor_tensor(Wl[:, slot, :], wf[:, k % 2, :], Wh[:, slot, :].bitcast(F32), ALU.subtract)\
                   .then_inc(w_ready, 1)

            def add_up(it, g):
                for m in range(KD):
                    dve.wait_ge(y_ready, it * 16 + (FREE_Y + KD * g + m + 1))
                    dve.wait_ge(y_added, it * 16 + (KD * g + m + 1))
                    dve.tensor_tensor(x[:, m, :], x[:, m, :], bank[4 + m % 4][:, :], ALU.add).then_inc(y_added, 1)

            weigh(0, 0, True)
            weigh(0, 1, True)
            with dve.Fori(0, NCH // 4 - 1) as it:
                weigh(it, 2)
                weigh(it, 3)
                add_up(it, 0)
                weigh(it, 4)
                weigh(it, 5)
                add_up(it, 1)
            weigh(NCH // 4 - 1, 2)
            weigh(NCH // 4 - 1, 3)
            add_up(NCH // 4 - 1, 0)
            add_up(NCH // 4 - 1, 1)


RETRIEVE_STEPS = 2 * (2 * (4 + 8 + 4 + 3) + 2 + 4 + 8 + 4 + 4 + 2 + 1 + 2 + 2 + 3 + 1 + 1)

_OUT = "out_dram"


def _constants(np):
    c = np.zeros((P, N_CONST), np.float32)
    p = np.arange(P)
    c[:, C_ID:C_ID + P] = np.eye(P)
    c[:, C_MASK + 3 * P:C_MASK + 4 * P] = np.where(p[None, :] <= p[:, None], 0.0, -1.0e30)
    c[:, C_IOTA:C_IOTA + P] = p[None, :]
    c[:, C_BLOCK:C_BLOCK + P] = p[:, None] // DH == p[None, :] // DH
    c[:, C_ONES:C_ONES + P] = 1.0
    for g, w in enumerate(WINDOWS):
        c[:, C_CNT + PAD * g:C_CNT + PAD * (g + 1)] = 1.0 / np.minimum(np.arange(PAD) + 1, w)
    c[:, C_EPS] = 1.0
    return c


def kernel(x, norm1_g, w_in, b_forget, q_norm_g, k_norm_g, w_pool, pool_scale, w_out,
           norm2_g, w_query, peer_sub_keys, expert_u, expert_v):
    import numpy as np
    import concourse.bacc as bacc
    from concourse.bass_utils import run_bass_kernel_spmd

    a = {n: np.asarray(v) for n, v in dict(x=x, n1=norm1_g, wi=w_in, bf=b_forget, qg=q_norm_g, kg=k_norm_g,
                                           wp=w_pool, ps=pool_scale, wo=w_out, n2=norm2_g, wq=w_query,
                                           sk=peer_sub_keys, u=expert_u, v=expert_v).items()}

    def column_chunks(w):
        n = w.shape[1] // P
        return w.reshape(KD, P, n, P).transpose(2, 1, 0, 3).reshape(n, P, KD * P)

    wi = a["wi"][0]
    forget = np.concatenate([wi[:, 4 * T:], np.zeros((D, P - HEADS), wi.dtype)], axis=1)
    cols = column_chunks(wi[:, :4 * T])
    values = wi[:, 3 * T:4 * T].reshape(4, 2, P, T).transpose(0, 2, 1, 3).reshape(4, P, 2 * T)
    qk = [cols[o + c] for c in range(4) for o in (4, 8)]
    wst = np.concatenate([column_chunks(forget), values, np.stack(qk), cols[0:4], column_chunks(a["wo"][0]),
                          column_chunks(a["wq"][0])])
    per_channel = [a["n1"][0].reshape(8, P).T, a["n2"][0].reshape(8, P).T, a["qg"][0].reshape(4, P).T,
                   a["kg"][0].reshape(4, P).T, a["ps"][0].reshape(4, P).T,
                   np.pad(a["bf"][0], (0, P - HEADS))[:, None]]
    ins = {
        "xT": a["x"][0].T.reshape(KD, P, T).transpose(1, 0, 2),
        "wst": wst,
        "vecs": np.concatenate(per_channel, axis=1),
        "consts": _constants(np),
        "w_pool": a["wp"][0].transpose(1, 0, 2),
        "keysT": a["sk"][0].transpose(2, 0, 1),
        "uT": a["u"][0].reshape(NCH, P, KD, P).transpose(0, 3, 2, 1).reshape(NCH, P, D),
        "v": a["v"][0].reshape(NCH, P, D),
    }
    ins = {n + "_dram": np.ascontiguousarray(v) for n, v in ins.items()}
    nc = bacc.Bacc("TRN2", target_bir_lowering=False, num_devices=1)
    aps = [nc.dram_tensor(n, v.shape, mybir.dt.from_np(v.dtype), kind="ExternalInput").ap() for n, v in ins.items()]
    aps.append(nc.dram_tensor(_OUT, (P, KD, T), F32, kind="ExternalOutput").ap())
    program(nc, *aps)
    got = run_bass_kernel_spmd(nc, [ins], core_ids=[0]).results[0][_OUT]
    return got.transpose(1, 0, 2).reshape(D, T).T.reshape(1, T, D)
```

```python
import concourse.bass as bass
from concourse import mybir
from contextlib import ExitStack

F32 = mybir.dt.float32
F32R = mybir.dt.float32r
U32 = mybir.dt.uint32
ALU = mybir.AluOpType
ACT = mybir.ActivationFunctionType
AX = mybir.AxisListType

P = 128
T = 512
D = 1024
KD = D // P
TB = T // P
HEADS, DH = 8, 64
WINDOWS = (2, 4, 8, 16)
PH = 8
TOPK = 16
NKEY = 128
NCH = 128
PAD = 16
EPS = 1e-6
LOWEST = -3.0e38

VALUES = (0, 1, 3, 4)
F_W, Q_W = 2, 5
POOL_W, OUT_W, EARLY_W = 13, 17, 25
UP_EARLY = 4
QUERY_W = EARLY_W + UP_EARLY
RAW, SPLIT = 2, 2
ROUND_Q, ROUND_U = 4, 8
ROUND_W = ROUND_Q + ROUND_U
ROUNDS = 2 * PH // ROUND_Q
UP_RETR = ROUNDS * ROUND_U
SOFT_TURNS = (1, 1, 1)
UP_SOFT = 2 * sum(SOFT_TURNS)
UP_GATE = 16
UP_REST = 6
STORED = UP_EARLY + UP_RETR + UP_SOFT + UP_GATE + UP_REST
SOFT_W = QUERY_W + ROUNDS * ROUND_W
GATE_W = SOFT_W + UP_SOFT
REST_W = GATE_W + UP_GATE
EXP_W = REST_W + UP_REST
U_LAG = SOFT_W - (UP_EARLY + UP_RETR)
BODIES = NCH - STORED >> 1
GROUP = 4
GROUPS = T // GROUP // UP_GATE
GATE_TURNS = UP_GATE // TB // 2
PIECES = 4
PIECE = NCH // PIECES

C_ID, C_MASK, C_IOTA, C_BLOCK, C_ONES, C_CNT, C_EPS = 0, 128, 256, 384, 512, 640, 704
N_CONST = 705
G1, G2, QG, KG, PS, BF = 0, 8, 16, 20, 24, 28
N_VEC = 29


def program(nc, xT, wst, vecs, consts, w_pool, keysT, uT, v, out):
    g_dram = nc.dram_tensor("gates_dram", (NCH, P, T), F32, kind="Internal").ap()
    a_dram = nc.dram_tensor("a_dram", (STORED, P, T), F32, kind="Internal").ap()
    f_dram = nc.dram_tensor("forget_dram", (HEADS, T), F32, kind="Internal").ap()
    ctx = ExitStack()
    with ctx:
        def sb(name, shape, dt=F32, where=ctx):
            return where.enter_context(nc.sbuf_tensor(name, shape, dt))

        def sem(name):
            return ctx.enter_context(nc.semaphore(name))

        cst = sb("cst", [P, N_CONST])
        vec = sb("vec", [P, N_VEC])
        x = sb("x", [P, KD, T])
        hh = sb("hh", [P, KD, T], F32R)
        hl = sb("hl", [P, KD, T], F32R)
        raw = sb("raw", [P, RAW, D])
        wh = sb("wh", [P, SPLIT, D], F32R)
        wl = sb("wl", [P, SPLIT, D], F32R)
        act_a = sb("act_a", [P, 2, T])

        norms = ExitStack()
        root = sb("root", [P, T], where=norms)
        var = sb("var", [P, T], where=norms)
        rinv = sb("rinv", [P, T], where=norms)
        norms.close()
        slotT = sb("slotT", [P, 3, T])

        mixers = ExitStack()
        mh = sb("mh", [P, KD, T], F32R, mixers)
        ml = sb("ml", [P, KD, T], F32R, mixers)
        qn = sb("qn", [P, 4, T], where=mixers)
        kn = sb("kn", [P, 4, T], where=mixers)
        vs = sb("vs", [P, TB, T], where=mixers)
        pr = sb("pr", [P, 2, TB, T], where=mixers)
        pT = sb("pT", [P, 2, 1280], where=mixers)
        nf = sb("nf", [P, 2, T], where=mixers)
        zc = sb("zc", [P, 2, T], where=mixers)
        sq = sb("sq", [P, 2, T], where=mixers)
        pad = sb("pad", [P, 3, PAD + T], where=mixers)
        pm = sb("pm", [P, T], where=mixers)
        newt = sb("newt", [P, T], where=mixers)
        fg = sb("fg", [HEADS, 3, T], where=mixers)
        rmax = sb("rmax", [P, 2, TB], where=mixers)
        nmax = sb("nmax", [P, 2, TB], where=mixers)
        rsum = sb("rsum", [P, 2, TB], where=mixers)
        rrec = sb("rrec", [P, 2, TB], where=mixers)
        wp = sb("wp", [P, 4, P], where=mixers)
        mixers.close()

        retr = ExitStack()
        keys = sb("keys", [P, 2, NKEY], where=retr)
        qh = sb("qh", [P, 2, T], where=retr)
        sc = sb("sc", [P, 4, TB, NKEY], where=retr)
        sc2 = sb("sc2", [P, TB, NKEY], where=retr)
        kv = sb("kv", [P, 2, TB, TOPK], where=retr)
        ku = sb("ku", [P, 2, TB, TOPK], U32, where=retr)
        kf = sb("kf", [P, 2, TB, TOPK], where=retr)
        cand = sb("cand", [P, TB, TOPK, TOPK], where=retr)
        cand2 = sb("cand2", [P, TB, TOPK * TOPK], where=retr)
        tv = sb("tv", [P, TB, TOPK], where=retr)
        pos = sb("pos", [P, TB, TOPK], U32, where=retr)
        ab = sb("ab", [P, 2, TB, TOPK], U32, where=retr)
        abf = sb("abf", [P, 2, TB, TOPK], where=retr)
        hit = sb("hit", [P, 2, TB, TOPK, TOPK], where=retr)
        hit2 = sb("hit2", [P, 2, TB, TOPK, TOPK], where=retr)
        best = sb("best", [P, TB, PH, TOPK], where=retr)
        ge = sb("ge", [P, TB, PH, TOPK], where=retr)
        tick = sb("tick", [P, 1], where=retr)
        gs = sb("gs", [P, TB, PH], where=retr)
        gr = sb("gr", [P, TB, PH], where=retr)
        sel = sb("sel", [P, 3, TB, PH, TOPK], where=retr)
        retr.close()

        gate = ExitStack()
        gbuf = sb("gbuf", [P, 2, NCH, P], where=gate)
        ohb = sb("ohb", [P, 2, 4, P], where=gate)
        oha = sb("oha", [P, 2, 4, P], where=gate)
        gate.close()

        exp = ExitStack()
        vraw = sb("vraw", [P, 2, D], where=exp)
        vh = sb("vh", [P, 4, D], F32R, exp)
        vl = sb("vl", [P, 4, D], F32R, exp)
        gt = sb("gt", [P, 2, T], where=exp)
        old_a = sb("old_a", [P, 2, T], where=exp)
        wf = sb("wf", [P, 2, T], where=exp)
        Wh = sb("Wh", [P, 4, T], F32R, exp)
        Wl = sb("Wl", [P, 4, T], F32R, exp)
        exp.close()

        bank = [ctx.enter_context(nc.psum_tensor(f"bank{i}", [P, T], F32)) for i in range(8)]
        GP = 2
        SS, PV = 2, 3
        S_BANK, PT_BANK = 4, 6

        ident = cst[:, C_ID:C_ID + P]
        iota = cst[:, C_IOTA:C_IOTA + P]
        block_ones = cst[:, C_BLOCK:C_BLOCK + P]
        ones = cst[:, C_ONES:C_ONES + P]
        mask = cst[:, C_MASK:C_MASK + P]

        in_consts, in_pool, in_keys = sem("in_consts"), sem("in_pool"), sem("in_keys")
        in_x = [sem(f"in_x{i}") for i in range(4)]
        raw_in = [sem(f"raw_in{i}") for i in range(RAW)]
        w_hi, w_lo, w_used = sem("w_hi"), sem("w_lo"), sem("w_used")
        sq_ready, sq_used = sem("sq_ready"), sem("sq_used")
        var_ready, ln_ready, root_ready = sem("var_ready"), sem("ln_ready"), sem("root_ready")
        h_ready, h_hi, h_lo = sem("h_ready"), sem("h_hi"), sem("h_lo")
        g_ready, g_hi, g_lo = sem("g_ready"), sem("g_hi"), sem("g_lo")
        early_scaled, early_done = sem("early_scaled"), sem("early_done")
        zc_ready, zc_used, v_saved = sem("zc_ready"), sem("zc_used"), sem("v_saved")
        f_taken, f_abs, f_ln, f_done, f_stored = (sem("f_taken"), sem("f_abs"), sem("f_ln"), sem("f_done"),
                                                  sem("f_stored"))
        nf_in = [sem("nf_in0"), sem("nf_in1")]
        s_ready, s_masked, e_ready, p_scaled = sem("s_ready"), sem("s_masked"), sem("e_ready"), sem("p_scaled")
        pt_ready, pt_saved, pv_ready = sem("pt_ready"), sem("pt_saved"), sem("pv_ready")
        att_hi, att_lo = sem("att_hi"), sem("att_lo")
        pool_prod, pool_hi, pool_lo, x1_ready = sem("pool_prod"), sem("pool_hi"), sem("pool_lo"), sem("x1_ready")
        out_done = sem("out_done")
        sc_prod, sc_ready, sc_used = sem("sc_prod"), sem("sc_ready"), sem("sc_used")
        gd_ready, ge_ready, sel_ready = sem("gd_ready"), sem("ge_ready"), sem("sel_ready")
        tr_ready, tr_saved = sem("tr_ready"), sem("tr_saved")
        oh_ready, oh_used, gp_used = sem("oh_ready"), sem("oh_used"), sem("gp_used")
        gp_stored = [sem("gp_stored0"), sem("gp_stored1")]
        a_out = [sem("a_out0"), sem("a_out1")]
        at_in = [sem("at_in0"), sem("at_in1")]
        w_ready, v_hi, v_lo = sem("w_ready"), sem("v_hi"), sem("v_lo")
        y_ready, y_added = sem("y_ready"), sem("y_added")
        vraw_in = [sem("vraw_in0"), sem("vraw_in1")]
        gt_in = [sem("gt_in0"), sem("gt_in1")]
        dve_done = sem("dve_done")
        stored = sem("stored")

        FREE_BANKS, FREE_SC, FREE_OH, FREE_A, FREE_V, FREE_W, FREE_Y, FREE_SUM = 2, 4, 2, 16, 2, 2, 2 * KD, KD

        qk = [("proj", Q_W + i) for i in range(8)]
        ss = [("ss", i) for i in range(8)]
        stages = [("norm1", 0)] + [("proj", n) for n in range(Q_W)]
        stages += [qk[0], qk[1], ss[0], qk[2], ss[1], qk[3], ss[2], ("score", 0)]
        fill = [[qk[4], ss[3]], [qk[5], ss[4]], [qk[6], ss[5]], [qk[7], ss[6]], [ss[7], ("proj", POOL_W)],
                [("proj", POOL_W + 1), ("poolmix", 0)], [("proj", POOL_W + 2), ("poolmix", 1)],
                [("proj", POOL_W + 3), ("poolmix", 2)]]
        for h in range(HEADS):
            stages += [("score", h + 1)] * (h + 1 < HEADS) + fill[h] + [("attend", h)]
        stages += [("poolmix", 3)] + [("proj", OUT_W + m) for m in range(KD)] + [("norm2", 0), ("early", 0)]

        def kind(n):
            return ("f" if n == F_W else "v" if n < Q_W else "qk" if n < POOL_W else "pool" if n < OUT_W else "out")

        def bank_of(n):
            return n % 2

        def taken(n):
            return {"f": (f_taken, 1), "qk": (zc_ready, n - Q_W + 1), "pool": (zc_ready, n - Q_W + 1),
                    "out": (x1_ready, n - OUT_W + 1)}[kind(n)]

        SQ_QK, SQ_OUT = KD, 2 * KD
        PT_AT = ((0, 512), (512, 384), (896, 384))
        KEY_AT = (0, 512, 896, 1152)

        block = ctx.enter_context(nc.Block())

        @block.sync
        def _(sp):
            for i in range(4):
                sp.dma_start(x[:, 2 * i:2 * i + 2, :], xT[:, 2 * i:2 * i + 2, :]).then_inc(in_x[i], 16)
                if i == 0:
                    sp.dma_start(cst[:, :], consts).then_inc(in_consts, 16)
                    sp.dma_start(vec[:, :], vecs).then_inc(in_consts, 16)

            for n in range(QUERY_W):
                if n == 4:
                    sp.dma_start(wp[:, :, :], w_pool).then_inc(in_pool, 16)
                if n == 9:
                    sp.wait_ge(f_done, 1)
                    sp.dma_start(f_dram, fg[:, 2, :]).then_inc(f_stored, 16)
                    sp.wait_ge(f_stored, 16)
                if 9 <= n < 9 + HEADS:
                    h = n - 9
                    if h >= 2:
                        sp.wait_ge(s_masked, TB * (h - 1))
                    sp.dma_start(nf[:, h % 2, :], f_dram[h:h + 1, :].broadcast_to([P, T])).then_inc(nf_in[h % 2], 16)
                if n >= RAW:
                    sp.wait_ge(w_lo, n - RAW + 1)
                sp.dma_start(raw[:, n % RAW, :], wst[n] if n < EARLY_W else uT[n - EARLY_W])\
                  .then_inc(raw_in[n % RAW], 16)

            def load_w(n, static, src):
                sp.wait_ge(w_lo, n - (RAW - 1))
                sp.dma_start(raw[:, static % RAW, :], src.rearrange("a p n -> p (a n)"))\
                  .then_inc(raw_in[static % RAW], 16)

            with sp.Fori(0, ROUNDS) as it:
                for k in range(ROUND_Q):
                    n = QUERY_W + 3 * k
                    load_w(it * ROUND_W + n, n, wst[bass.ds(it * ROUND_Q + (EARLY_W + k), 1)])
                    for j in range(2):
                        load_w(it * ROUND_W + (n + 1 + j), n + 1 + j, uT[bass.ds(it * ROUND_U + (UP_EARLY + 2 * k + j), 1)])
            def load_u(n, static, row):
                load_w(n, static, uT[bass.ds(row, 1)])

            with sp.Fori(0, UP_SOFT // 2) as it:
                for j in range(2):
                    load_u(it * 2 + (SOFT_W + j), SOFT_W + j, it * 2 + (UP_EARLY + UP_RETR + j))
            for j in range(2):
                load_w(GATE_W + j, GATE_W + j, uT[GATE_W + j - U_LAG:GATE_W + j - U_LAG + 1])
            for b in range(TB + 1):
                if b:
                    sp.wait_ge(gp_used, FREE_BANKS + P // GROUP * b)
                with sp.Fori(0, GATE_TURNS) as it:
                    for j in range(2):
                        n = GATE_W + 2 * GATE_TURNS * b + j + 2
                        load_u(it * 2 + n, n, it * 2 + (n - U_LAG))
                        if b:
                            part, frames = bass.ds(it * (2 * PIECE) + PIECE * j, PIECE), slice((b - 1) * P, b * P)
                            sp.dma_start(g_dram[part, :, frames].rearrange("i j t -> j i t"),
                                         gbuf[:, (b - 1) % 2, part, :]).then_inc(gp_stored[(b - 1) % 2], 16)
            for n in range(GATE_W + 2 * GATE_TURNS * (TB + 1) + 2, EXP_W + 2):
                load_w(n, n, uT[n - U_LAG:n - U_LAG + 1])
            for half in range(2):
                sp.wait_ge(gp_stored[half], 16 * PIECES * TB // 2)
            for j in range(2):
                sp.wait_ge(a_out[j], FREE_A + 16 * (STORED // 2))

            def load_down(it, g, j):
                c, q = it * 2 + (g * STORED + j), it * 4 + (2 * g + j)
                sp.wait_ge(v_lo, q + 1)
                sp.dma_start(vraw[:, j, :], v[bass.ds(c, 1)].rearrange("a p n -> p (a n)")).then_inc(vraw_in[j], 16)
                sp.wait_ge(w_ready, q + 1)
                sp.dma_start(gt[:, j, :], g_dram[bass.ds(c, 1)].rearrange("a p n -> p (a n)")).then_inc(gt_in[j], 16)
                if g == 0:
                    sp.dma_start(old_a[:, j, :], a_dram[bass.ds(c, 1)].rearrange("a p n -> p (a n)"))\
                      .then_inc(at_in[j], 16)

            def body(it, last=False):
                load_down(it, 0, 0)
                load_down(it, 0, 1)
                if not last:
                    for j in range(2):
                        load_w(it * 2 + (EXP_W + 2 + j), EXP_W + j, uT[bass.ds(it * 2 + (STORED + 2 + j), 1)])
                load_down(it, 1, 0)
                load_down(it, 1, 1)

            with sp.Fori(0, BODIES - 1) as it:
                body(it)
            body(BODIES - 1, last=True)
            sp.wait_ge(y_added, FREE_SUM + KD * (NCH // 2))
            sp.dma_start(out, x[:, :, :]).then_inc(stored, 16)
            sp.wait_ge(stored, 16)

        @block.gpsimd
        def _(pool):
            def split_lo(n, slot_raw, slot):
                pool.wait_ge(w_hi, n + 1)
                pool.tensor_tensor(wl[:, slot, :], raw[:, slot_raw, :], wh[:, slot, :].bitcast(F32), ALU.subtract)\
                    .then_inc(w_lo, 1)

            def split_v(it, g, j):
                s = 2 * g + j
                pool.wait_ge(v_hi, it * 4 + (s + 1))
                pool.tensor_tensor(vl[:, s, :], vraw[:, j, :], vh[:, s, :].bitcast(F32), ALU.subtract)\
                    .then_inc(v_lo, 1)

            for n in range(QUERY_W):
                split_lo(n, n % RAW, n % SPLIT)
            with pool.Fori(0, ROUNDS) as it:
                for k in range(ROUND_W):
                    split_lo(it * ROUND_W + (QUERY_W + k), (QUERY_W + k) % RAW, (QUERY_W + k) % SPLIT)
            with pool.Fori(0, (EXP_W - SOFT_W) // 2) as it:
                for j in range(2):
                    split_lo(it * 2 + (SOFT_W + j), (SOFT_W + j) % RAW, (SOFT_W + j) % SPLIT)
            for j in range(2):
                split_lo(EXP_W + j, (EXP_W + j) % RAW, (EXP_W + j) % SPLIT)
            pool.sem_inc(v_lo, FREE_V)

            def body(it, last=False):
                for g in range(2):
                    for j in range(2):
                        split_v(it, g, j)
                    if g == 0 and not last:
                        for j in range(2):
                            split_lo(it * 2 + (EXP_W + 2 + j), (EXP_W + j) % RAW, (EXP_W + j) % SPLIT)

            with pool.Fori(0, BODIES - 1) as it:
                body(it)
            body(BODIES - 1, last=True)

        @block.scalar
        def _(act):
            def split_hi(n, static, round_):
                act.wait_ge(raw_in[static % RAW], round_ * 16)
                if static >= SPLIT:
                    act.wait_ge(w_used, n - (SPLIT - 1))
                act.activation(wh[:, static % SPLIT, :], raw[:, static % RAW, :], ACT.Copy).then_inc(w_hi, 1)

            def square(i, src):
                if i >= 2:
                    act.wait_ge(sq_used, i - 1)
                act.activation(sq[:, i % 2, :], src, ACT.Square).then_inc(sq_ready, 1)

            roots = 0
            for what, i in stages:
                if what == "norm1":
                    for k in range(KD):
                        act.wait_ge(in_x[k // 2], 16)
                        square(k, x[:, k, :])
                elif what == "proj":
                    n = i
                    if kind(n) == "f":
                        act.wait_ge(f_abs, 1)
                        act.activation(fg[:, 1, :], fg[:, 1, :], ACT.Exp).then_inc(f_ln, 1)
                        act.wait_ge(f_ln, 1)
                        act.wait_ge(in_consts, 32)
                        act.activation(fg[:, 1, :], fg[:, 1, :], ACT.Ln, bias=cst[0:HEADS, C_EPS:C_EPS + 1])\
                           .then_inc(f_ln, 1)
                    elif kind(n) in ("qk", "pool"):
                        z = n - Q_W
                        act.wait_ge(w_used, n + 1)
                        if z >= 2:
                            act.wait_ge(zc_used, z - 1)
                        elif z == 0:
                            act.wait_ge(h_lo, KD)
                        act.activation(zc[:, z % 2, :], bank[bank_of(n)][:, :], ACT.Copy).then_inc(zc_ready, 1)
                        if kind(n) == "qk":
                            act.wait_ge(zc_ready, z + 1)
                            square(SQ_QK + z, zc[:, z % 2, :])
                    elif kind(n) == "out":
                        m = n - OUT_W
                        act.wait_ge(x1_ready, m + 1)
                        square(SQ_OUT + m, x[:, m, :])
                        act.wait_ge(g_ready, m + 1)
                        act.activation(mh[:, m, :], zc[:, m % 2, :], ACT.Copy).then_inc(g_hi, 1)
                    split_hi(n + 2, n + 2, (n + 2) // RAW + 1)
                elif what == "poolmix":
                    act.wait_ge(pool_prod, i + 1)
                    act.wait_ge(in_consts, 32)
                    act.activation(hh[:, i, :], bank[SS][:, :], ACT.Copy, scale=vec[:, PS + i:PS + i + 1])\
                       .then_inc(pool_hi, 1)
                elif what == "score":
                    for b in range(TB):
                        act.wait_ge(s_masked, TB * i + b + 1)
                        act.activation(pr[:, i % 2, b, 0:(b + 1) * P], pr[:, i % 2, b, 0:(b + 1) * P], ACT.Exp,
                                       bias=nmax[:, i % 2, b:b + 1], accum_out=rsum[:, i % 2, b:b + 1])\
                           .then_inc(e_ready, 1)
                elif what == "attend":
                    for g, (at, size) in enumerate(PT_AT):
                        act.wait_ge(pt_ready, 3 * i + g + 1)
                        if i >= 2:
                            act.wait_ge(pv_ready, i - 1)
                        act.activation(pT[:, i % 2, at:at + size], bank[PT_BANK + (3 * i + g) % 2][:, 0:size],
                                       ACT.Copy).then_inc(pt_saved, 1)
                    rows = slice(DH * (i % 2), DH * (i % 2) + DH)
                    act.wait_ge(pv_ready, i + 1)
                    act.activation(hh[rows, 4 + i // 2, :], bank[PV][rows, :], ACT.Copy).then_inc(att_hi, 1)
                if what in ("norm1", "ss", "norm2"):
                    act.wait_ge(var_ready, roots + 1)
                    act.activation(root[:, :], var[:, :], ACT.Ln).then_inc(ln_ready, 1)
                    act.wait_ge(ln_ready, roots + 1)
                    act.activation(root[:, :], root[:, :], ACT.Exp, scale=-0.5).then_inc(root_ready, 1)
                    roots += 1
                if what in ("norm1", "norm2"):
                    base, dst = (0, mh) if what == "norm1" else (KD, hh)
                    for k in range(KD):
                        if what == "norm1" and k in (0, 2):
                            split_hi(k // 2, k // 2, 1)
                        act.wait_ge(h_ready, base + k + 1)
                        if what == "norm2" and k == 0:
                            act.wait_ge(w_used, EARLY_W)
                        act.activation(dst[:, k, :], zc[:, k % 2, :], ACT.Copy).then_inc(h_hi, 1)
                        if what == "norm2" and k in (3, 6):
                            n = EARLY_W + k // 3 + 1
                            split_hi(n, n, n // RAW + 1)
                if what == "early":
                    for j in range(2):
                        act.sem_inc(a_out[j], FREE_A)
                    for i in range(UP_EARLY):
                        if i % 2 == 0:
                            n = QUERY_W + i // 2
                            split_hi(n, n, n // RAW + 1)
                        act.wait_ge(early_scaled, i + 1)
                        act.wait_ge(a_out[i % 2], 16 * (i // 2) + FREE_A)
                        act.activation(act_a[:, i % 2, :], bank[S_BANK + i][:, :], ACT.Gelu).then_inc(early_done, 1)
                        act.wait_ge(early_done, i + 1)
                        act.dma_start(a_dram[i], act_a[:, i % 2, :]).then_inc(a_out[i % 2], 16)
                    act.dma_start(keys[:, :, :], keysT).then_inc(in_keys, 16)

            act.sem_inc(out_done, FREE_BANKS)
            act.sem_inc(sc_ready, FREE_BANKS)

            def next_hi(n, static, rounds):
                split_hi(n + 2, static + 2, rounds + ((static + 2) // RAW + 1))

            def gelu(n, static, slot):
                act.wait_ge(w_used, n + 1)
                act.activation(act_a[:, slot, :], bank[static % 2][:, :], ACT.Gelu).then_inc(out_done, 1)

            def up_stored(n, static, rounds, turn, j):
                act.wait_ge(a_out[j], turn * 16 + FREE_A)
                gelu(n, static, j)
                next_hi(n, static, rounds)
                act.wait_ge(out_done, n + (FREE_BANKS + 1 - QUERY_W))
                act.dma_start(a_dram[bass.ds(turn * 2 + j, 1)].rearrange("a p n -> p (a n)"), act_a[:, j, :])\
                   .then_inc(a_out[j], 16)

            with act.Fori(0, ROUNDS) as it:
                for k in range(ROUND_Q):
                    n = QUERY_W + 3 * k
                    rounds = it * (ROUND_W // RAW)
                    act.wait_ge(w_used, it * ROUND_W + (n + 1))
                    act.activation(qh[:, k % 2, :], bank[n % 2][:, :], ACT.Copy).then_inc(out_done, 1)
                    next_hi(it * ROUND_W + n, n, rounds)
                    for j in range(2):
                        up_stored(it * ROUND_W + (n + 1 + j), n + 1 + j, rounds, it * (ROUND_U // 2) + (UP_EARLY // 2 + k), j)
                    act.wait_ge(sc_prod, it * ROUND_Q + (k + 1))
                    act.wait_ge(sc_used, it * ROUND_Q + (k + 1))
                    act.activation(sc[:, k, :, :].rearrange("p b k -> p (b k)"), bank[S_BANK + k % 2][:, :], ACT.Copy)\
                       .then_inc(sc_ready, 1)

            def ups_stored(first, turns):
                with act.Fori(0, turns) as it:
                    for j in range(2):
                        up_stored(it * 2 + (first + j), first + j, it, it + (first - U_LAG) // 2, j)

            ups_stored(SOFT_W, SOFT_TURNS[0])
            act.wait_ge(gd_ready, 1)
            act.activation(ge[:, :, :, :], best[:, :, :, :], ACT.Exp).then_inc(ge_ready, 1)
            ups_stored(SOFT_W + 2 * SOFT_TURNS[0], SOFT_TURNS[1])
            for a in range(3):
                act.wait_ge(tr_ready, a + 1)
                act.activation(slotT[:, a, :], bank[PT_BANK + a % 2][:, :], ACT.Copy).then_inc(tr_saved, 1)
            ups_stored(SOFT_W + 2 * sum(SOFT_TURNS[:2]), SOFT_TURNS[2])

            act.sem_inc(gp_used, FREE_BANKS)
            for b in range(TB):
                if b >= 2:
                    act.wait_ge(gp_stored[b % 2], 16 * PIECES)
                with act.Fori(0, GATE_TURNS) as it:
                    for j in range(2):
                        for k in range(GROUPS):
                            group = GROUPS * j + k
                            act.wait_ge(oh_used, it * (2 * GROUPS) + (FREE_OH + P // GROUP * b + group + 1))
                            act.activation(gbuf[:, b % 2, :, bass.ds(it * (2 * GROUPS * GROUP) + GROUP * group, GROUP)],
                                           bank[GP + k % 2][:, :].rearrange("j (t i) -> j i t", t=GROUP), ACT.Copy)\
                               .then_inc(gp_used, 1)
                        n = GATE_W + 2 * GATE_TURNS * b + j
                        up_stored(it * 2 + n, n, it, it + (n - j - U_LAG) // 2, j)
            ups_stored(REST_W, UP_REST // 2)

            for j in range(2):
                act.wait_ge(a_out[j], FREE_A + 16 * (STORED // 2))

            def split_v(it, g, j):
                s = 2 * g + j
                act.wait_ge(vraw_in[j], it * 32 + 16 * (g + 1))
                act.wait_ge(y_ready, it * 16 + KD * (g + 1))
                act.activation(vh[:, s, :], vraw[:, j, :], ACT.Copy).then_inc(v_hi, 1)

            def body(it, last=False):
                split_v(it, 0, 0)
                split_v(it, 0, 1)
                for j in range(2):
                    act.wait_ge(w_ready, it * 4 + (j + 1))
                    gelu(it * 2 + (EXP_W + j), EXP_W + j, j)
                    if not last:
                        next_hi(it * 2 + (EXP_W + j), EXP_W + j, it)
                split_v(it, 1, 0)
                split_v(it, 1, 1)

            with act.Fori(0, BODIES - 1) as it:
                body(it)
            body(BODIES - 1, last=True)

        @block.tensor
        def _(pe):
            def three(dst, ah, al, bh, bl, start, stop):
                pe.matmul(dst, ah, bh, start=start, stop=False)
                pe.matmul(dst, ah, bl, start=False, stop=False)
                return pe.matmul(dst, al, bh, start=False, stop=stop)

            def project(dst, s, right_h, right_l, between=None):
                for k in range(KD):
                    if between is not None:
                        between(k)
                    last = three(dst, wh[:, s, k * P:(k + 1) * P], wl[:, s, k * P:(k + 1) * P],
                                 right_h[:, k, :], right_l[:, k, :], k == 0, k == KD - 1)
                last.then_inc(w_used, 1)

            def sum_square(i, weights, start, stop):
                pe.wait_ge(sq_ready, i + 1)
                pe.matmul(bank[SS][:, :], weights, sq[:, i % 2, :], start=start, stop=stop).then_inc(sq_used, 1)

            pe.wait_ge(in_consts, 32)
            last_in_bank = {}
            for what, i in stages:
                if what == "norm1":
                    for k in range(KD):
                        sum_square(k, ones, k == 0, k == KD - 1)
                elif what == "proj":
                    n, kd = i, kind(i)
                    pe.wait_ge(w_lo, n + 1)
                    if kd == "v":
                        pair = VALUES.index(n)
                        pe.wait_ge(h_lo, 2 * pair + 2)
                        for b in range(TB):
                            for kk in range(2):
                                k = 2 * pair + kk
                                at, w = slice(b * P, (b + 1) * P), slice(kk * T, (kk + 1) * T)
                                last = three(bank[S_BANK + b][:, :], mh[:, k, at], ml[:, k, at],
                                             wh[:, n % SPLIT, w], wl[:, n % SPLIT, w], k == 0, k == KD - 1)
                        last.then_inc(w_used, 1)
                        continue
                    if bank_of(n) in last_in_bank:
                        pe.wait_ge(*taken(last_in_bank[bank_of(n)]))
                    last_in_bank[bank_of(n)] = n
                    if n == F_W:
                        pe.wait_ge(h_lo, KD)
                    if n == OUT_W:
                        pe.wait_ge(att_lo, HEADS)
                        pe.wait_ge(pool_lo, 4)
                    project(bank[bank_of(n)][:, :], n % SPLIT, *((hh, hl) if kd == "out" else (mh, ml)))
                    if n > OUT_W:
                        sum_square(SQ_OUT + n - OUT_W - 1, ones, n == OUT_W + 1, False)
                elif what == "ss":
                    pe.wait_ge(var_ready, 1 + i)
                    sum_square(SQ_QK + i, block_ones, True, True)
                elif what == "poolmix":
                    pe.wait_ge(zc_used, 9 + i)
                    if i:
                        pe.wait_ge(pool_lo, i)
                    else:
                        pe.wait_ge(var_ready, 9)
                        pe.wait_ge(in_pool, 16)
                    pe.matmul(bank[SS][:, :], wp[:, i, :], pm[:, :], start=True, stop=True).then_inc(pool_prod, 1)
                elif what == "score":
                    h, c = i, i // 2
                    rows = slice(DH * (h % 2), DH * (h % 2) + DH)
                    pe.wait_ge(zc_used, 2 * c + 2)
                    for b in range(TB):
                        n = TB * h + b
                        if n >= 2:
                            pe.wait_ge(s_masked, n - 1)
                        else:
                            pe.wait_ge(v_saved, TB)
                        pe.matmul(bank[S_BANK + n % 2][:, 0:(b + 1) * P], qn[rows, c, b * P:(b + 1) * P],
                                  kn[rows, c, 0:(b + 1) * P], start=True, stop=True).then_inc(s_ready, 1)
                elif what == "attend":
                    h = i
                    pe.wait_ge(p_scaled, TB * (h + 1))
                    for g, pieces in enumerate(([(0, b) for b in range(4)], [(1, b) for b in range(1, 4)],
                                                [(2, 2), (2, 3), (3, 3)])):
                        n = 3 * h + g
                        if n >= 2:
                            pe.wait_ge(pt_saved, n - 1)
                        for at, (key, b) in enumerate(pieces):
                            last = pe.transpose(bank[PT_BANK + n % 2][:, at * P:(at + 1) * P],
                                                pr[:, h % 2, b, key * P:(key + 1) * P], ident)
                        last.then_inc(pt_ready, 1)
                    pe.wait_ge(pt_saved, 3 * h + 3)
                    if h:
                        pe.wait_ge(att_lo, h)
                    for key in range(TB):
                        size = (TB - key) * P
                        last = pe.matmul(bank[PV][:, key * P:T], vs[:, key, (h // 2) * P:(h // 2 + 1) * P],
                                         pT[:, h % 2, KEY_AT[key]:KEY_AT[key] + size],
                                         start=(key == 0), stop=(key == TB - 1))
                    last.then_inc(pv_ready, 1)
                elif what == "norm2":
                    sum_square(SQ_OUT + KD - 1, ones, False, True)
                elif what == "early":
                    for i in range(UP_EARLY):
                        pe.wait_ge(w_lo, EARLY_W + i + 1)
                        project(bank[S_BANK + i][:, :], (EARLY_W + i) % SPLIT, mh, ml,
                                (lambda k: pe.wait_ge(g_lo, k + 1)) if i == 0 else None)

            pe.wait_ge(h_lo, 2 * KD)
            pe.wait_ge(in_keys, 16)

            def turn(n, static, between=None):
                pe.wait_ge(w_lo, n + 1)
                pe.wait_ge(out_done, n + (1 - QUERY_W))
                project(bank[static % 2][:, :], static % SPLIT, hh, hl, between)

            def scores(it, k):
                pe.wait_ge(early_done, UP_EARLY)
                pe.wait_ge(out_done, it * ROUND_W + (FREE_BANKS + 3 * k + 1))
                pe.wait_ge(sc_ready, it * ROUND_Q + (k + 1))
                for b in range(TB):
                    last = pe.matmul(bank[S_BANK + k % 2][:, b * P:(b + 1) * P], qh[:, k % 2, b * P:(b + 1) * P],
                                     keys[:, k % 2, :], start=True, stop=True)
                last.then_inc(sc_prod, 1)

            with pe.Fori(0, ROUNDS) as it:
                for k in range(ROUND_Q):
                    for j in range(3):
                        n = QUERY_W + 3 * k + j
                        turn(it * ROUND_W + n, n)
                    scores(it, k)

            def turns(first, count):
                with pe.Fori(0, count) as it:
                    for j in range(2):
                        turn(it * 2 + (first + j), first + j)

            turns(SOFT_W, sum(SOFT_TURNS[:2]))
            pe.wait_ge(sel_ready, 1)
            for a in range(3):
                if a == 2:
                    pe.wait_ge(tr_saved, 1)
                for b in range(TB):
                    last = pe.transpose(bank[PT_BANK + a % 2][:, b * P:(b + 1) * P],
                                        sel[:, a, b, :, :].rearrange("p h k -> p (h k)"), ident)
                last.then_inc(tr_ready, 1)
            turns(SOFT_W + 2 * sum(SOFT_TURNS[:2]), SOFT_TURNS[2])

            pe.sem_inc(oh_used, FREE_OH)
            with pe.Fori(0, UP_GATE // 2) as it:
                for j in range(2):
                    def frames(k):
                        group = it * (2 * GROUPS) + (GROUPS * j + k)
                        pe.wait_ge(oh_ready, group + 1)
                        pe.wait_ge(gp_used, group + 1)
                        for t in range(GROUP):
                            last = pe.matmul(bank[GP + k % 2][:, t * P:(t + 1) * P], ohb[:, k % 2, t, :],
                                             oha[:, k % 2, t, :], start=True, stop=True)
                        last.then_inc(oh_used, 1)

                    turn(it * 2 + (GATE_W + j), GATE_W + j, frames)
            turns(REST_W, UP_REST // 2)

            pe.sem_inc(y_ready, FREE_Y)

            def down(it, g):
                pe.wait_ge(w_ready, it * 4 + (FREE_W + 2 * g + 2))
                pe.wait_ge(v_lo, it * 4 + (FREE_V + 2 * g + 2))
                for m in range(KD):
                    pe.wait_ge(y_added, it * 16 + (KD * g + m - 3 + FREE_SUM))
                    for j in range(2):
                        s, at_ = 2 * g + j, slice(m * P, (m + 1) * P)
                        last = three(bank[4 + m % 4][:, :], vh[:, s, at_], vl[:, s, at_], Wh[:, s, :], Wl[:, s, :],
                                     j == 0, j == 1)
                    last.then_inc(y_ready, 1)

            with pe.Fori(0, BODIES) as it:
                for j in range(2):
                    turn(it * 2 + (EXP_W + j), EXP_W + j)
                down(it, 0)
                down(it, 1)

        @block.vector
        def _(dve):
            base, count = 0, 0

            def lo_part(i, k, hi_done, lo_done, high, low):
                dve.wait_ge(hi_done, i + 1)
                dve.tensor_tensor(low[:, k, :], zc[:, k % 2, :], high[:, k, :].bitcast(F32), ALU.subtract)\
                   .then_inc(lo_done, 1)

            def step(instruction):
                nonlocal count
                count += 1
                instruction.then_inc(dve_done, 1)

            def fence():
                dve.wait_ge(dve_done, base + count)

            def fence_apart():
                dve.drain()

            for i in range(3):
                step(dve.memset(pad[:, i, 0:PAD], 0.0))
            dve.wait_ge(in_consts, 32)
            for i in range(4):
                dve.wait_ge(in_x[i], 16)
            roots = 0
            for what, i in stages:
                if what in ("norm1", "ss", "norm2"):
                    scale, eps = {"norm1": (1.0 / D, EPS), "norm2": (1.0 / D, EPS),
                                  "ss": (1.0, DH * EPS) if i % 2 == 0 else (1.0 / DH, EPS)}[what]
                    dve.wait_ge(sq_used, {"norm1": KD, "ss": SQ_QK + i + 1, "norm2": 3 * KD}[what])
                    fence()
                    dve.tensor_scalar(var[:, :], bank[SS][:, :], scale, eps, ALU.mult, ALU.add).then_inc(var_ready, 1)
                    dve.wait_ge(root_ready, roots + 1)
                    roots += 1
                    step(dve.tensor_tensor(newt[:, :], root[:, :], root[:, :], ALU.mult))
                    fence()
                    step(dve.tensor_tensor(newt[:, :], newt[:, :], var[:, :], ALU.mult))
                    fence()
                    step(dve.tensor_scalar(newt[:, :], newt[:, :], -0.5, 1.5, ALU.mult, ALU.add))
                    fence()
                    step(dve.tensor_tensor(rinv[:, :], newt[:, :], root[:, :], ALU.mult))
                    fence()
                if what == "ss":
                    n, c = i, i // 2
                    dst, g = (qn, QG) if i % 2 == 0 else (kn, KG)
                    dve.scalar_tensor_tensor(dst[:, c, :], zc[:, n % 2, :], vec[:, g + c:g + c + 1], rinv[:, :],
                                             ALU.mult, ALU.mult).then_inc(zc_used, 1)
                    dve.wait_ge(zc_used, i + 1)
                elif what in ("norm1", "norm2"):
                    first, g, high, low = (0, G1, mh, ml) if what == "norm1" else (KD, G2, hh, hl)
                    for k in range(KD):
                        if k >= 2:
                            dve.wait_ge(h_lo, first + k - 1)
                        elif first:
                            dve.wait_ge(g_lo, KD)
                        dve.scalar_tensor_tensor(zc[:, k % 2, :], x[:, k, :], vec[:, g + k:g + k + 1], rinv[:, :],
                                                 ALU.mult, ALU.mult).then_inc(h_ready, 1)
                        if k:
                            lo_part(first + k - 1, k - 1, h_hi, h_lo, high, low)
                    lo_part(first + KD - 1, KD - 1, h_hi, h_lo, high, low)
                elif what == "early":
                    for i in range(UP_EARLY):
                        dve.wait_ge(w_used, EARLY_W + i + 1)
                        dve.tensor_tensor(bank[S_BANK + i][:, :], bank[S_BANK + i][:, :], rinv[:, :], ALU.mult)\
                           .then_inc(early_scaled, 1)
                elif what == "proj":
                    n, kd = i, kind(i)
                    if kd == "f":
                        dve.wait_ge(w_used, F_W + 1)
                        dve.tensor_scalar(fg[:, 0, :], bank[bank_of(n)][0:HEADS, :], vec[0:HEADS, BF:BF + 1], None,
                                          ALU.add).then_inc(f_taken, 1)
                        dve.wait_ge(f_taken, 1)
                        dve.scalar_tensor_tensor(fg[:, 1, :], fg[:, 0, :], -1.0, fg[:, 0, :], ALU.mult, ALU.min)\
                           .then_inc(f_abs, 1)
                        dve.wait_ge(f_ln, 2)
                        step(dve.scalar_tensor_tensor(fg[:, 0, :], fg[:, 0, :], 0.0, fg[:, 1, :],
                                                      ALU.min, ALU.subtract))
                        fence()
                        step(dve.tensor_scalar(fg[:, 0, :], fg[:, 0, :], -1.0, None, ALU.mult))
                        fence()
                        dve.tensor_tensor_scan(fg[:, 2, :], fg[:, 0, :], fg[:, 1, :], 0.0, ALU.add, ALU.bypass)\
                           .then_inc(f_done, 1)
                    elif n == Q_W - 1:
                        dve.wait_ge(w_used, Q_W)
                        for b in range(TB):
                            dve.tensor_copy(vs[:, b, :], bank[S_BANK + b][:, :]).then_inc(v_saved, 1)
                    elif kd == "pool":
                        g, z = n - POOL_W, n - Q_W
                        w = WINDOWS[g]
                        dve.wait_ge(zc_ready, z + 1)
                        fence()
                        step(dve.tensor_copy(pad[:, 0, PAD:], zc[:, z % 2, :]))
                        src, s = 0, 1
                        while s < w:
                            fence()
                            dst = 2 if src == 1 else 1
                            step(dve.tensor_tensor(pad[:, dst, PAD:], pad[:, src, PAD:],
                                                   pad[:, src, PAD - s:PAD + T - s], ALU.add))
                            src, s = dst, 2 * s
                        fence()
                        if g:
                            dve.wait_ge(pool_prod, g)
                        step(dve.scalar_tensor_tensor(pm[:, :], pad[:, src, PAD:], 1.0 / w, zc[:, z % 2, :],
                                                      ALU.mult, ALU.subtract))
                        fence()
                        step(dve.tensor_tensor(pm[:, 0:PAD], pad[:, src, PAD:2 * PAD],
                                               cst[:, C_CNT + PAD * g:C_CNT + PAD * (g + 1)], ALU.mult))
                        fence()
                        dve.tensor_tensor(pm[:, 0:PAD], pm[:, 0:PAD], zc[:, z % 2, 0:PAD], ALU.subtract)\
                           .then_inc(zc_used, 1)
                    elif kd == "out":
                        m = n - OUT_W
                        dve.wait_ge(w_used, n + 1)
                        dve.tensor_tensor(x[:, m, :], x[:, m, :], bank[bank_of(n)][:, :], ALU.add)\
                           .then_inc(x1_ready, 1)
                        if m == 0:
                            dve.wait_ge(zc_used, 12)
                        if m >= 2:
                            dve.wait_ge(g_lo, m - 1)
                        dve.wait_ge(x1_ready, m + 1)
                        dve.tensor_scalar(zc[:, m % 2, :], x[:, m, :], vec[:, G2 + m:G2 + m + 1], None, ALU.mult)\
                           .then_inc(g_ready, 1)
                        lo_part(m, m, g_hi, g_lo, mh, ml)
                elif what == "poolmix":
                    dve.wait_ge(pool_hi, i + 1)
                    dve.scalar_tensor_tensor(hl[:, i, :], bank[SS][:, :], vec[:, PS + i:PS + i + 1],
                                             hh[:, i, :].bitcast(F32), ALU.mult, ALU.subtract).then_inc(pool_lo, 1)
                elif what == "score":
                    h = i
                    dve.wait_ge(nf_in[h % 2], 16 * (h // 2 + 1))
                    if h >= 2:
                        dve.wait_ge(pt_ready, 3 * (h - 1))
                    for b in range(TB):
                        s = bank[S_BANK + (TB * h + b) % 2]
                        size = (b + 1) * P
                        dve.wait_ge(s_ready, TB * h + b + 1)
                        step(dve.tensor_tensor(s[:, b * P:size], s[:, b * P:size], mask, ALU.add))
                        fence()
                        step(dve.tensor_tensor_reduce(pr[:, h % 2, b, 0:size], s[:, 0:size], nf[:, h % 2, 0:size],
                                                      1.0, LOWEST, ALU.add, ALU.max, rmax[:, h % 2, b:b + 1]))
                        fence()
                        dve.tensor_scalar(nmax[:, h % 2, b:b + 1], rmax[:, h % 2, b:b + 1], -1.0, None, ALU.mult)\
                           .then_inc(s_masked, 1)
                    dve.wait_ge(e_ready, TB * (h + 1))
                    step(dve.reciprocal(rrec[:, h % 2, :], rsum[:, h % 2, :]))
                    fence()
                    for b in range(TB):
                        size = (b + 1) * P
                        dve.tensor_scalar(pr[:, h % 2, b, 0:size], pr[:, h % 2, b, 0:size], rrec[:, h % 2, b:b + 1],
                                          None, ALU.mult).then_inc(p_scaled, 1)
                elif what == "attend":
                    rows = slice(DH * (i % 2), DH * (i % 2) + DH)
                    dve.wait_ge(att_hi, i + 1)
                    dve.tensor_tensor(hl[rows, 4 + i // 2, :], bank[PV][rows, :],
                                      hh[rows, 4 + i // 2, :].bitcast(F32), ALU.subtract).then_inc(att_lo, 1)

            dve.sem_inc(sc_used, FREE_SC)
            fence()
            before = count
            with dve.Fori(0, ROUNDS) as it:
                base, count = it * RETRIEVE_STEPS + before, 0
                for k in range(4):
                    half = k % 2
                    kt, ku_ = kv[:, half], ku[:, half]
                    s = sc[:, k]
                    dve.wait_ge(sc_ready, it * ROUND_Q + (FREE_BANKS + k + 1))
                    dve.memset(tick[:, :], 0.0)
                    fence_apart()
                    for b in range(TB):
                        step(dve.max(kt[:, b, 0:8], s[:, b, :]))
                    fence_apart()
                    for b in range(TB):
                        step(dve.max_index(ku_[:, b, 0:8], kt[:, b, 0:8], s[:, b, :]))
                        step(dve.match_replace(sc2[:, b, :], kt[:, b, 0:8], s[:, b, :], LOWEST))
                    fence_apart()
                    for b in range(TB):
                        ins = dve.max(kt[:, b, 8:16], sc2[:, b, :])
                        step(ins)
                    fence_apart()
                    for b in range(TB):
                        ins = dve.max_index(ku_[:, b, 8:16], kt[:, b, 8:16], sc2[:, b, :])
                        if b < TB - 1:
                            step(ins)
                        else:
                            ins.then_inc(sc_used, 1)
                    if half == 0:
                        continue
                    h = it * 2 + k // 2
                    dve.wait_ge(sc_used, it * 4 + (FREE_SC + k + 1))
                    wide = [P, TB, TOPK, TOPK]
                    step(dve.tensor_tensor(cand[:, :, :, :], kv[:, 0].unsqueeze(3).broadcast_to(wide),
                                           kv[:, 1].unsqueeze(2).broadcast_to(wide), ALU.add))
                    step(dve.tensor_copy(kf[:, :, :, :], ku[:, :, :, :]))
                    fence_apart()
                    flat = cand[:, :, :, :].rearrange("p b i j -> p b (i j)")
                    for b in range(TB):
                        step(dve.max(tv[:, b, 0:8], flat[:, b, :]))
                    fence_apart()
                    for b in range(TB):
                        step(dve.max_index(pos[:, b, 0:8], tv[:, b, 0:8], flat[:, b, :]))
                        step(dve.match_replace(cand2[:, b, :], tv[:, b, 0:8], flat[:, b, :], LOWEST))
                    fence_apart()
                    for b in range(TB):
                        step(dve.max(tv[:, b, 8:16], cand2[:, b, :]))
                    fence_apart()
                    for b in range(TB):
                        step(dve.max_index(pos[:, b, 8:16], tv[:, b, 8:16], cand2[:, b, :]))
                    fence()
                    step(dve.tensor_copy(best[:, :, bass.ds(h, 1), :].rearrange("p b a k -> p b (a k)"), tv[:, :, :]))
                    step(dve.tensor_scalar(ab[:, 0], pos[:, :, :], 4, None, ALU.logical_shift_right))
                    step(dve.tensor_scalar(ab[:, 1], pos[:, :, :], 15, None, ALU.bitwise_and))
                    fence()
                    step(dve.tensor_copy(abf[:, :, :, :], ab[:, :, :, :]))
                    fence()
                    for a in range(2):
                        step(dve.tensor_tensor(hit[:, a], abf[:, a].unsqueeze(3).broadcast_to(wide),
                                               iota[:, 0:TOPK].unsqueeze(1).unsqueeze(1).broadcast_to(wide),
                                               ALU.is_equal))
                    fence()
                    for a in range(2):
                        step(dve.tensor_tensor(hit2[:, a], hit[:, a], kf[:, a].unsqueeze(2).broadcast_to(wide),
                                               ALU.mult))
                    fence()
                    for a in range(2):
                        step(dve.tensor_reduce(sel[:, a, :, bass.ds(h, 1), :].rearrange("p b a k -> p b (a k)"),
                                               hit2[:, a], AX.X, ALU.add))
                assert count == RETRIEVE_STEPS, count
            base, count = 0, before + RETRIEVE_STEPS * ROUNDS
            fence()
            narrow = [P, TB * PH, TOPK]
            flat_best, flat_e = (a[:, :, :, :].rearrange("p b h k -> p (b h) k") for a in (best, ge))
            flat_s, flat_r = (a[:, :, :].rearrange("p b h -> p (b h)") for a in (gs, gr))
            step(dve.tensor_copy(flat_s, flat_best[:, :, 0:1].rearrange("p n a -> p (n a)")))
            fence()
            dve.tensor_tensor(flat_best, flat_best, flat_s.unsqueeze(2).broadcast_to(narrow), ALU.subtract)\
               .then_inc(gd_ready, 1)
            dve.wait_ge(ge_ready, 1)
            step(dve.tensor_reduce(flat_s, flat_e, AX.X, ALU.add))
            fence()
            step(dve.reciprocal(flat_r, flat_s))
            fence()
            dve.tensor_tensor(sel[:, 2, :, :, :].rearrange("p b h k -> p (b h) k"), flat_e,
                              flat_r.unsqueeze(2).broadcast_to(narrow), ALU.mult).then_inc(sel_ready, 1)

            dve.wait_ge(tr_saved, 3)
            with dve.Fori(0, T // 8) as it:
                for k in range(2):
                    dve.wait_ge(oh_used, it * 2 + (k + 1))
                    at = bass.ds(it * 8 + 4 * k, 4)
                    dve.tensor_tensor(ohb[:, k], iota.unsqueeze(1).broadcast_to([P, 4, P]),
                                      slotT[:, 1, at].unsqueeze(2).broadcast_to([P, 4, P]), ALU.is_equal)
                    for t in range(4):
                        one = bass.ds(it * 8 + (4 * k + t), 1)
                        last = dve.tensor_scalar(oha[:, k, t, :], iota, slotT[:, 0, one], slotT[:, 2, one],
                                                 ALU.is_equal, ALU.mult)
                    last.then_inc(oh_ready, 1)

            dve.sem_inc(y_added, FREE_SUM)
            dve.sem_inc(w_ready, FREE_W)
            before = count

            def weigh(it, g, j):
                s = 2 * g + j
                if g == 0:
                    dve.wait_ge(at_in[j], it * 16 + 16)
                    a = old_a[:, j, :]
                else:
                    dve.wait_ge(out_done, it * 2 + (FREE_BANKS + EXP_W - QUERY_W + j + 1))
                    a = act_a[:, j, :]
                dve.wait_ge(gt_in[j], it * 32 + 16 * (g + 1))
                dve.wait_ge(w_ready, it * 4 + (s + 1))
                dve.tensor_tensor(wf[:, j, :], gt[:, j, :], a, ALU.mult).then_inc(dve_done, 1)
                dve.wait_ge(y_ready, it * 16 + KD * (g + 1))
                dve.wait_ge(dve_done, it * 8 + (before + 2 * s + 1))
                dve.tensor_copy(Wh[:, s, :], wf[:, j, :]).then_inc(dve_done, 1)
                dve.wait_ge(dve_done, it * 8 + (before + 2 * s + 2))
                dve.tensor_tensor(Wl[:, s, :], wf[:, j, :], Wh[:, s, :].bitcast(F32), ALU.subtract)\
                   .then_inc(w_ready, 1)

            def add_up(it, g):
                for m in range(KD):
                    dve.wait_ge(y_ready, it * 16 + (FREE_Y + KD * g + m + 1))
                    dve.wait_ge(y_added, it * 16 + (KD * g + m + 1))
                    dve.tensor_tensor(x[:, m, :], x[:, m, :], bank[4 + m % 4][:, :], ALU.add).then_inc(y_added, 1)

            with dve.Fori(0, BODIES) as it:
                for g in range(2):
                    weigh(it, g, 0)
                    weigh(it, g, 1)
                add_up(it, 0)
                add_up(it, 1)


RETRIEVE_STEPS = 2 * (2 * (4 + 8 + 4 + 3) + 2 + 4 + 8 + 4 + 4 + 3 + 1 + 2 + 2 + 2)

_OUT = "out_dram"


def _constants(np):
    c = np.zeros((P, N_CONST), np.float32)
    p = np.arange(P)
    c[:, C_ID:C_ID + P] = np.eye(P)
    c[:, C_MASK:C_MASK + P] = np.where(p[None, :] <= p[:, None], 0.0, -1.0e30)
    c[:, C_IOTA:C_IOTA + P] = p[None, :]
    c[:, C_BLOCK:C_BLOCK + P] = p[:, None] // DH == p[None, :] // DH
    c[:, C_ONES:C_ONES + P] = 1.0
    for g, w in enumerate(WINDOWS):
        c[:, C_CNT + PAD * g:C_CNT + PAD * (g + 1)] = 1.0 / np.minimum(np.arange(PAD) + 1, w)
    c[:, C_EPS] = 1.0
    return c


def kernel(x, norm1_g, w_in, b_forget, q_norm_g, k_norm_g, w_pool, pool_scale, w_out,
           norm2_g, w_query, peer_sub_keys, expert_u, expert_v):
    import numpy as np
    import concourse.bacc as bacc
    from concourse.bass_utils import run_bass_kernel_spmd

    a = {n: np.asarray(v) for n, v in dict(x=x, n1=norm1_g, wi=w_in, bf=b_forget, qg=q_norm_g, kg=k_norm_g,
                                           wp=w_pool, ps=pool_scale, wo=w_out, n2=norm2_g, wq=w_query,
                                           sk=peer_sub_keys, u=expert_u, v=expert_v).items()}

    def column_chunks(w):
        n = w.shape[1] // P
        return w.reshape(KD, P, n, P).transpose(2, 1, 0, 3).reshape(n, P, KD * P)

    wi = a["wi"][0]
    forget = np.concatenate([wi[:, 4 * T:], np.zeros((D, P - HEADS), wi.dtype)], axis=1)
    cols = column_chunks(wi[:, :4 * T])
    values = wi[:, 3 * T:4 * T].reshape(4, 2, P, T).transpose(0, 2, 1, 3).reshape(4, P, 2 * T)
    qk = [cols[o + c] for c in range(4) for o in (4, 8)]
    wst = np.concatenate([values[:2], column_chunks(forget), values[2:], np.stack(qk), cols[0:4], column_chunks(a["wo"][0]),
                          column_chunks(a["wq"][0])])
    per_channel = [a["n1"][0].reshape(8, P).T, a["n2"][0].reshape(8, P).T, a["qg"][0].reshape(4, P).T,
                   a["kg"][0].reshape(4, P).T, a["ps"][0].reshape(4, P).T,
                   np.pad(a["bf"][0], (0, P - HEADS))[:, None]]
    ins = {
        "xT": a["x"][0].T.reshape(KD, P, T).transpose(1, 0, 2),
        "wst": wst,
        "vecs": np.concatenate(per_channel, axis=1),
        "consts": _constants(np),
        "w_pool": a["wp"][0].transpose(1, 0, 2),
        "keysT": a["sk"][0].transpose(2, 0, 1),
        "uT": a["u"][0].reshape(NCH, P, KD, P).transpose(0, 3, 2, 1).reshape(NCH, P, D),
        "v": a["v"][0].reshape(NCH, P, D),
    }
    ins = {n + "_dram": np.ascontiguousarray(v) for n, v in ins.items()}
    nc = bacc.Bacc("TRN2", target_bir_lowering=False, num_devices=1,
                   dynamic_dma_scratch_size=1024)
    aps = [nc.dram_tensor(n, v.shape, mybir.dt.from_np(v.dtype), kind="ExternalInput").ap() for n, v in ins.items()]
    aps.append(nc.dram_tensor(_OUT, (P, KD, T), F32, kind="ExternalOutput").ap())
    program(nc, *aps)
    got = run_bass_kernel_spmd(nc, [ins], core_ids=[0]).results[0][_OUT]
    return got.transpose(1, 0, 2).reshape(D, T).T.reshape(1, T, D)
```

```python
import concourse.bass as bass
from concourse import mybir
from contextlib import ExitStack

F32 = mybir.dt.float32
F32R = mybir.dt.float32r
U32 = mybir.dt.uint32
ALU = mybir.AluOpType
ACT = mybir.ActivationFunctionType
AX = mybir.AxisListType

P = 128
T = 512
D = 1024
KD = D // P
TB = T // P
HEADS, DH = 8, 64
WINDOWS = (2, 4, 8, 16)
PH = 8
TOPK = 16
NKEY = 128
NCH = 128
PAD = 16
EPS = 1e-6
LOWEST = -3.0e38

VALUES = (0, 1, 2, 3)
F_W = 4
QK_W = tuple(range(5, 13))
POOL_W, OUT_W, EARLY_W = 13, 17, 25
UP_EARLY = 4
QUERY_W = EARLY_W + UP_EARLY
RAW, SPLIT = 2, 2
ROUND_Q, ROUND_U = 4, 8
ROUND_W = ROUND_Q + ROUND_U
ROUNDS = 2 * PH // ROUND_Q
UP_RETR = ROUNDS * ROUND_U
SOFT_TURNS = (1, 1, 1)
UP_SOFT = 2 * sum(SOFT_TURNS)
UP_GATE = 16
UP_REST = 6
STORED = UP_EARLY + UP_RETR + UP_SOFT + UP_GATE + UP_REST
SOFT_W = QUERY_W + ROUNDS * ROUND_W
GATE_W = SOFT_W + UP_SOFT
REST_W = GATE_W + UP_GATE
EXP_W = REST_W + UP_REST
U_LAG = SOFT_W - (UP_EARLY + UP_RETR)
BODIES = NCH - STORED >> 1
GROUP = 4
GROUPS = T // GROUP // UP_GATE
GATE_TURNS = UP_GATE // TB // 2
PIECES = 4
PIECE = NCH // PIECES

C_ID, C_MASK, C_IOTA, C_BLOCK, C_ONES, C_CNT, C_EPS = 0, 128, 256, 384, 512, 640, 704
N_CONST = 705
G1, G2, QG, KG, PS, BF = 0, 8, 16, 20, 24, 28
N_VEC = 29


def program(nc, xT, wst, vecs, consts, w_pool, keysT, uT, v, out):
    g_dram = nc.dram_tensor("gates_dram", (NCH, P, T), F32, kind="Internal").ap()
    a_dram = nc.dram_tensor("a_dram", (STORED, P, T), F32, kind="Internal").ap()
    f_dram = nc.dram_tensor("forget_dram", (HEADS, T), F32, kind="Internal").ap()
    ctx = ExitStack()
    with ctx:
        def sb(name, shape, dt=F32, where=ctx):
            return where.enter_context(nc.sbuf_tensor(name, shape, dt))

        def sem(name):
            return ctx.enter_context(nc.semaphore(name))

        cst = sb("cst", [P, N_CONST])
        vec = sb("vec", [P, N_VEC])
        x = sb("x", [P, KD, T])
        hh = sb("hh", [P, KD, T], F32R)
        hl = sb("hl", [P, KD, T], F32R)
        raw = sb("raw", [P, RAW, D])
        wh = sb("wh", [P, SPLIT, D], F32R)
        wl = sb("wl", [P, SPLIT, D], F32R)
        act_a = sb("act_a", [P, 2, T])

        norms = ExitStack()
        root = sb("root", [P, T], where=norms)
        var = sb("var", [P, T], where=norms)
        rinv = sb("rinv", [P, T], where=norms)
        norms.close()
        slotT = sb("slotT", [P, 3, T])

        mixers = ExitStack()
        mh = sb("mh", [P, KD, T], F32R, mixers)
        ml = sb("ml", [P, KD, T], F32R, mixers)
        qn = sb("qn", [P, 4, T], where=mixers)
        kn = sb("kn", [P, 4, T], where=mixers)
        vs = sb("vs", [P, TB, T], where=mixers)
        pr = sb("pr", [P, 2, TB, T], where=mixers)
        pT = sb("pT", [P, 2, 1280], where=mixers)
        nf = sb("nf", [P, 2, T], where=mixers)
        zc = sb("zc", [P, 2, T], where=mixers)
        sq = sb("sq", [P, 4, T], where=mixers)
        pad = sb("pad", [P, 3, PAD + T], where=mixers)
        pm = sb("pm", [P, T], where=mixers)
        newt = sb("newt", [P, T], where=mixers)
        fg = sb("fg", [HEADS, 3, T], where=mixers)
        rcol = sb("rcol", [P, TB], where=mixers)
        rmax = sb("rmax", [P, 2, TB], where=mixers)
        nmax = sb("nmax", [P, 2, TB], where=mixers)
        rsum = sb("rsum", [P, 2, TB], where=mixers)
        rrec = sb("rrec", [P, 2, TB], where=mixers)
        wp = sb("wp", [P, 4, P], where=mixers)
        mixers.close()

        retr = ExitStack()
        keys = sb("keys", [P, 2, NKEY], where=retr)
        qh = sb("qh", [P, 2, T], where=retr)
        sc = sb("sc", [P, 4, TB, NKEY], where=retr)
        sc2 = sb("sc2", [P, TB, NKEY], where=retr)
        kv = sb("kv", [P, 2, TB, TOPK], where=retr)
        ku = sb("ku", [P, 2, TB, TOPK], U32, where=retr)
        kf = sb("kf", [P, 2, TB, TOPK], where=retr)
        cand = sb("cand", [P, TB, TOPK, TOPK], where=retr)
        cand2 = sb("cand2", [P, TB, TOPK * TOPK], where=retr)
        tv = sb("tv", [P, TB, TOPK], where=retr)
        pos = sb("pos", [P, TB, TOPK], U32, where=retr)
        ab = sb("ab", [P, 2, TB, TOPK], U32, where=retr)
        abf = sb("abf", [P, 2, TB, TOPK], where=retr)
        hit = sb("hit", [P, 2, TB, TOPK, TOPK], where=retr)
        hit2 = sb("hit2", [P, 2, TB, TOPK, TOPK], where=retr)
        best = sb("best", [P, TB, PH, TOPK], where=retr)
        ge = sb("ge", [P, TB, PH, TOPK], where=retr)
        tick = sb("tick", [P, 1], where=retr)
        gs = sb("gs", [P, TB, PH], where=retr)
        gr = sb("gr", [P, TB, PH], where=retr)
        sel = sb("sel", [P, 3, TB, PH, TOPK], where=retr)
        retr.close()

        gate = ExitStack()
        gbuf = sb("gbuf", [P, 2, NCH, P], where=gate)
        ohb = sb("ohb", [P, 2, 4, P], where=gate)
        oha = sb("oha", [P, 2, 4, P], where=gate)
        gate.close()

        exp = ExitStack()
        vraw = sb("vraw", [P, 2, D], where=exp)
        vh = sb("vh", [P, 4, D], F32R, exp)
        vl = sb("vl", [P, 4, D], F32R, exp)
        gt = sb("gt", [P, 2, T], where=exp)
        old_a = sb("old_a", [P, 2, T], where=exp)
        wf = sb("wf", [P, 2, T], where=exp)
        Wh = sb("Wh", [P, 4, T], F32R, exp)
        Wl = sb("Wl", [P, 4, T], F32R, exp)
        exp.close()

        bank = [ctx.enter_context(nc.psum_tensor(f"bank{i}", [P, T], F32)) for i in range(8)]
        GP = 2
        SS, PV = 2, 3
        S_BANK, PT_BANK = 4, 6

        ident = cst[:, C_ID:C_ID + P]
        iota = cst[:, C_IOTA:C_IOTA + P]
        block_ones = cst[:, C_BLOCK:C_BLOCK + P]
        ones = cst[:, C_ONES:C_ONES + P]
        mask = cst[:, C_MASK:C_MASK + P]

        in_consts, in_pool, in_keys = sem("in_consts"), sem("in_pool"), sem("in_keys")
        in_x = [sem(f"in_x{i}") for i in range(4)]
        raw_in = [sem(f"raw_in{i}") for i in range(RAW)]
        w_hi, w_lo, w_used = sem("w_hi"), sem("w_lo"), sem("w_used")
        sq_ready, sq_used = sem("sq_ready"), sem("sq_used")
        var_ready, ln_ready, root_ready = sem("var_ready"), sem("ln_ready"), sem("root_ready")
        h_ready, h_hi, h_lo = sem("h_ready"), sem("h_hi"), sem("h_lo")
        g_ready, g_hi, g_lo = sem("g_ready"), sem("g_hi"), sem("g_lo")
        col_prod, col_ready = sem("col_prod"), sem("col_ready")
        early_scaled, early_done = sem("early_scaled"), sem("early_done")
        zc_ready, zc_used, v_saved = sem("zc_ready"), sem("zc_used"), sem("v_saved")
        f_taken, f_abs, f_ln, f_done, f_stored = (sem("f_taken"), sem("f_abs"), sem("f_ln"), sem("f_done"),
                                                  sem("f_stored"))
        nf_in = [sem("nf_in0"), sem("nf_in1")]
        s_ready, s_masked, e_ready, p_scaled = sem("s_ready"), sem("s_masked"), sem("e_ready"), sem("p_scaled")
        pt_ready, pt_saved, pv_ready = sem("pt_ready"), sem("pt_saved"), sem("pv_ready")
        att_hi, att_lo = sem("att_hi"), sem("att_lo")
        pool_prod, pool_hi, pool_lo, x1_ready = sem("pool_prod"), sem("pool_hi"), sem("pool_lo"), sem("x1_ready")
        out_done = sem("out_done")
        sc_prod, sc_ready, sc_used = sem("sc_prod"), sem("sc_ready"), sem("sc_used")
        gd_ready, ge_ready, sel_ready = sem("gd_ready"), sem("ge_ready"), sem("sel_ready")
        tr_ready, tr_saved = sem("tr_ready"), sem("tr_saved")
        oh_ready, oh_used, gp_used = sem("oh_ready"), sem("oh_used"), sem("gp_used")
        gp_stored = [sem("gp_stored0"), sem("gp_stored1")]
        a_out = [sem("a_out0"), sem("a_out1")]
        at_in = [sem("at_in0"), sem("at_in1")]
        w_ready, v_hi, v_lo = sem("w_ready"), sem("v_hi"), sem("v_lo")
        y_ready, y_added = sem("y_ready"), sem("y_added")
        vraw_in = [sem("vraw_in0"), sem("vraw_in1")]
        gt_in = [sem("gt_in0"), sem("gt_in1")]
        dve_done = sem("dve_done")
        stored = sem("stored")

        FREE_BANKS, FREE_SC, FREE_OH, FREE_A, FREE_V, FREE_W, FREE_Y, FREE_SUM = 2, 4, 2, 16, 2, 2, 2 * KD, KD

        def score(h, at=(0, 0, 3, 5)):
            scores = [(k, "score", (h, b)) for b, k in enumerate(at)]
            scales = [(at[min(b + 2, 3)], "scale", (h, b)) for b in range(TB)]
            return scores[:3] + scales[:1] + scores[3:] + scales[1:]

        def head(h, n, *more):
            inner = list(more) + score(h + 1) + [(2, "transpose", (h, 2))]
            return [("transpose", (h, 0), []), ("transpose", (h, 1), []),
                    ("proj", n, sorted(inner, key=lambda item: item[0]))]

        def sums(i):
            return [(0, "ss", i), (1, "norm", i)]

        stages = [("norm1", 0, [])] + [("proj", n, []) for n in VALUES] + [("columns", 0, [])]
        stages += [("proj", F_W, []), ("proj", QK_W[0], []), ("proj", QK_W[1], sums(0))]
        stages += [("proj", QK_W[2], sums(1)), ("proj", QK_W[3], score(0, (4, 4, 5, 7)))]
        stages += head(0, QK_W[4], *sums(2)) + [("proj", QK_W[5], sums(3)), ("pv", 0, [])]
        stages += head(1, QK_W[6], *sums(4)) + [("pv", 1, [])]
        stages += head(2, QK_W[7], *sums(5)) + [("pv", 2, [])]
        stages += head(3, POOL_W, *sums(6)) + [("pv", 3, [])]
        stages += head(4, POOL_W + 1, *sums(7), (7, "mean", 0)) + [("pv", 4, [])]
        stages += head(5, POOL_W + 2, (6, "mean", 1), (6, "poolmix", 0)) + [("pv", 5, [])]
        stages += head(6, POOL_W + 3, (6, "mean", 2), (6, "poolmix", 1)) + [("pv", 6, [])]
        stages += [("poolmix", 2, []), ("transpose", (7, 0), []), ("transpose", (7, 1), []), ("mean", 3, [])]
        stages += [("transpose", (7, 2), []), ("pv", 7, []), ("poolmix", 3, [])]
        stages += [("proj", OUT_W + m, []) for m in range(KD)] + [("norm2", 0, []), ("early", 0, [])]
        in_turn = [s for what, i, inner in stages for s in [(w, j) for _, w, j in inner] + [(what, i)]]
        SCORED = [n for n in range(QUERY_W) for what, i, inner in stages
                  if (what, i) == ("proj", n) and any(w == "scale" for _, w, _ in inner)]

        def kind(n):
            return ("f" if n == F_W else "v" if n in VALUES else "qk" if n in QK_W else "pool" if n < OUT_W
                    else "out")

        def z_of(n):
            return QK_W.index(n) if n in QK_W else n - POOL_W + len(QK_W)

        def bank_of(n):
            return n % 2

        def taken(n):
            return {"f": (f_taken, 1), "out": (x1_ready, n - OUT_W + 1)}.get(kind(n)) or (zc_ready, z_of(n) + 1)

        SQ_QK, SQ_OUT = KD, 2 * KD
        PT_AT = ((0, 512), (512, 384), (896, 384))
        KEY_AT = (0, 512, 896, 1152)

        block = ctx.enter_context(nc.Block())

        @block.sync
        def _(sp):
            def load_x(i):
                sp.dma_start(x[:, 2 * i:2 * i + 2, :], xT[:, 2 * i:2 * i + 2, :]).then_inc(in_x[i], 16)

            load_x(0)
            sp.dma_start(cst[:, :], consts).then_inc(in_consts, 16)
            sp.dma_start(vec[:, :], vecs).then_inc(in_consts, 16)
            for n in range(QUERY_W):
                if n == 4:
                    sp.dma_start(wp[:, :, :], w_pool).then_inc(in_pool, 16)
                if n == SCORED[0] + 1:
                    sp.wait_ge(f_done, 1)
                    sp.dma_start(f_dram, fg[:, 2, :]).then_inc(f_stored, 16)
                    sp.wait_ge(f_stored, 16)
                for h in range(HEADS):
                    if n != max(SCORED[h], SCORED[0] + 1):
                        continue
                    if h >= 2:
                        sp.wait_ge(s_masked, TB * (h - 1))
                    sp.dma_start(nf[:, h % 2, :], f_dram[h:h + 1, :].broadcast_to([P, T])).then_inc(nf_in[h % 2], 16)
                if n >= RAW:
                    sp.wait_ge(w_lo, n - RAW + 1)
                sp.dma_start(raw[:, n % RAW, :], wst[n] if n < EARLY_W else uT[n - EARLY_W])\
                  .then_inc(raw_in[n % RAW], 16)
                if n == 0:
                    for i in range(1, 4):
                        load_x(i)

            def load_w(n, static, src):
                sp.wait_ge(w_lo, n - (RAW - 1))
                sp.dma_start(raw[:, static % RAW, :], src.rearrange("a p n -> p (a n)"))\
                  .then_inc(raw_in[static % RAW], 16)

            with sp.Fori(0, ROUNDS) as it:
                for k in range(ROUND_Q):
                    n = QUERY_W + 3 * k
                    load_w(it * ROUND_W + n, n, wst[bass.ds(it * ROUND_Q + (EARLY_W + k), 1)])
                    for j in range(2):
                        load_w(it * ROUND_W + (n + 1 + j), n + 1 + j, uT[bass.ds(it * ROUND_U + (UP_EARLY + 2 * k + j), 1)])
            def load_u(n, static, row):
                load_w(n, static, uT[bass.ds(row, 1)])

            with sp.Fori(0, UP_SOFT // 2) as it:
                for j in range(2):
                    load_u(it * 2 + (SOFT_W + j), SOFT_W + j, it * 2 + (UP_EARLY + UP_RETR + j))
            for j in range(2):
                load_w(GATE_W + j, GATE_W + j, uT[GATE_W + j - U_LAG:GATE_W + j - U_LAG + 1])
            for b in range(TB + 1):
                if b:
                    sp.wait_ge(gp_used, FREE_BANKS + P // GROUP * b)
                with sp.Fori(0, GATE_TURNS) as it:
                    for j in range(2):
                        n = GATE_W + 2 * GATE_TURNS * b + j + 2
                        load_u(it * 2 + n, n, it * 2 + (n - U_LAG))
                        if b:
                            part, frames = bass.ds(it * (2 * PIECE) + PIECE * j, PIECE), slice((b - 1) * P, b * P)
                            sp.dma_start(g_dram[part, :, frames].rearrange("i j t -> j i t"),
                                         gbuf[:, (b - 1) % 2, part, :]).then_inc(gp_stored[(b - 1) % 2], 16)
            for n in range(GATE_W + 2 * GATE_TURNS * (TB + 1) + 2, EXP_W + 2):
                load_w(n, n, uT[n - U_LAG:n - U_LAG + 1])
            for half in range(2):
                sp.wait_ge(gp_stored[half], 16 * PIECES * TB // 2)
            for j in range(2):
                sp.wait_ge(a_out[j], FREE_A + 16 * (STORED // 2))

            def load_down(it, g, j):
                c, q = it * 2 + (g * STORED + j), it * 4 + (2 * g + j)
                sp.wait_ge(v_lo, q + 1)
                sp.dma_start(vraw[:, j, :], v[bass.ds(c, 1)].rearrange("a p n -> p (a n)")).then_inc(vraw_in[j], 16)
                sp.wait_ge(w_ready, q + 1)
                sp.dma_start(gt[:, j, :], g_dram[bass.ds(c, 1)].rearrange("a p n -> p (a n)")).then_inc(gt_in[j], 16)
                if g == 0:
                    sp.dma_start(old_a[:, j, :], a_dram[bass.ds(c, 1)].rearrange("a p n -> p (a n)"))\
                      .then_inc(at_in[j], 16)

            def body(it, last=False):
                load_down(it, 0, 0)
                load_down(it, 0, 1)
                if not last:
                    for j in range(2):
                        load_w(it * 2 + (EXP_W + 2 + j), EXP_W + j, uT[bass.ds(it * 2 + (STORED + 2 + j), 1)])
                load_down(it, 1, 0)
                load_down(it, 1, 1)

            with sp.Fori(0, BODIES - 1) as it:
                body(it)
            body(BODIES - 1, last=True)
            for m in range(KD):
                sp.wait_ge(y_added, FREE_SUM + KD * (NCH // 2 - 1) + m + 1)
                sp.dma_start(out[:, m, :], x[:, m, :]).then_inc(stored, 16)
            sp.wait_ge(stored, 16 * KD)

        @block.gpsimd
        def _(pool):
            def split_lo(n, slot_raw, slot):
                pool.wait_ge(w_hi, n + 1)
                pool.tensor_tensor(wl[:, slot, :], raw[:, slot_raw, :], wh[:, slot, :].bitcast(F32), ALU.subtract)\
                    .then_inc(w_lo, 1)

            def split_v(it, g, j):
                s = 2 * g + j
                pool.wait_ge(v_hi, it * 4 + (s + 1))
                pool.tensor_tensor(vl[:, s, :], vraw[:, j, :], vh[:, s, :].bitcast(F32), ALU.subtract)\
                    .then_inc(v_lo, 1)

            for n in range(QUERY_W):
                split_lo(n, n % RAW, n % SPLIT)
            with pool.Fori(0, ROUNDS) as it:
                for k in range(ROUND_W):
                    split_lo(it * ROUND_W + (QUERY_W + k), (QUERY_W + k) % RAW, (QUERY_W + k) % SPLIT)
            with pool.Fori(0, (EXP_W - SOFT_W) // 2) as it:
                for j in range(2):
                    split_lo(it * 2 + (SOFT_W + j), (SOFT_W + j) % RAW, (SOFT_W + j) % SPLIT)
            for j in range(2):
                split_lo(EXP_W + j, (EXP_W + j) % RAW, (EXP_W + j) % SPLIT)
            pool.sem_inc(v_lo, FREE_V)

            def body(it, last=False):
                for g in range(2):
                    for j in range(2):
                        split_v(it, g, j)
                    if g == 0 and not last:
                        for j in range(2):
                            split_lo(it * 2 + (EXP_W + 2 + j), (EXP_W + j) % RAW, (EXP_W + j) % SPLIT)

            with pool.Fori(0, BODIES - 1) as it:
                body(it)
            body(BODIES - 1, last=True)

        @block.scalar
        def _(act):
            def split_hi(n, static, round_):
                act.wait_ge(raw_in[static % RAW], round_ * 16)
                if static >= SPLIT:
                    act.wait_ge(w_used, n - (SPLIT - 1))
                act.activation(wh[:, static % SPLIT, :], raw[:, static % RAW, :], ACT.Copy).then_inc(w_hi, 1)

            def square(i, src):
                if i >= 4:
                    act.wait_ge(sq_used, i - 3)
                act.activation(sq[:, i % 4, :], src, ACT.Square).then_inc(sq_ready, 1)

            roots = 0
            for what, i in in_turn:
                if what == "norm1":
                    for k in range(KD):
                        act.wait_ge(in_x[k // 2], 16)
                        square(k, x[:, k, :])
                        act.wait_ge(g_ready, k + 1)
                        act.activation(hh[:, k, :], zc[:, k % 2, :], ACT.Copy).then_inc(g_hi, 1)
                        if k in (1, 7):
                            split_hi(k // 7, k // 7, 1)
                elif what == "proj":
                    n = i
                    if n >= 2:
                        split_hi(n + 2, n + 2, (n + 2) // RAW + 1)
                    if kind(n) == "f":
                        act.wait_ge(f_abs, 1)
                        act.activation(fg[:, 1, :], fg[:, 1, :], ACT.Exp).then_inc(f_ln, 1)
                        act.wait_ge(f_ln, 1)
                        act.wait_ge(in_consts, 32)
                        act.activation(fg[:, 1, :], fg[:, 1, :], ACT.Ln, bias=cst[0:HEADS, C_EPS:C_EPS + 1])\
                           .then_inc(f_ln, 1)
                    elif kind(n) in ("qk", "pool"):
                        z = z_of(n)
                        act.wait_ge(w_used, n + 1)
                        if z >= 2:
                            act.wait_ge(zc_used, z - 1)
                        elif z == 0:
                            act.wait_ge(h_lo, KD)
                        act.activation(zc[:, z % 2, :], bank[bank_of(n)][:, :], ACT.Copy).then_inc(zc_ready, 1)
                        if kind(n) == "qk":
                            act.wait_ge(zc_ready, z + 1)
                            square(SQ_QK + z, zc[:, z % 2, :])
                    elif kind(n) == "out":
                        m = n - OUT_W
                        act.wait_ge(x1_ready, m + 1)
                        square(SQ_OUT + m, x[:, m, :])
                        act.wait_ge(g_ready, KD + m + 1)
                        act.activation(mh[:, m, :], zc[:, m % 2, :], ACT.Copy).then_inc(g_hi, 1)
                elif what == "poolmix":
                    act.wait_ge(pool_prod, i + 1)
                    act.wait_ge(in_consts, 32)
                    act.activation(hh[:, i, :], bank[SS][:, :], ACT.Copy, scale=vec[:, PS + i:PS + i + 1])\
                       .then_inc(pool_hi, 1)
                elif what == "score":
                    h, b = i
                    act.wait_ge(s_masked, TB * h + b + 1)
                    act.activation(pr[:, h % 2, b, 0:(b + 1) * P], pr[:, h % 2, b, 0:(b + 1) * P], ACT.Exp,
                                   bias=nmax[:, h % 2, b:b + 1], accum_out=rsum[:, h % 2, b:b + 1])\
                       .then_inc(e_ready, 1)
                elif what == "transpose":
                    h, g = i
                    at, size = PT_AT[g]
                    act.wait_ge(pt_ready, 3 * h + g + 1)
                    if h >= 2:
                        act.wait_ge(pv_ready, h - 1)
                    act.activation(pT[:, h % 2, at:at + size], bank[PT_BANK + (3 * h + g) % 2][:, 0:size],
                                   ACT.Copy).then_inc(pt_saved, 1)
                elif what == "pv":
                    rows = slice(DH * (i % 2), DH * (i % 2) + DH)
                    act.wait_ge(pv_ready, i + 1)
                    act.activation(hh[rows, 4 + i // 2, :], bank[PV][rows, :], ACT.Copy).then_inc(att_hi, 1)
                if what in ("norm1", "ss", "norm2"):
                    act.wait_ge(var_ready, roots + 1)
                    act.activation(root[:, :], var[:, :], ACT.Ln).then_inc(ln_ready, 1)
                    act.wait_ge(ln_ready, roots + 1)
                    act.activation(root[:, :], root[:, :], ACT.Exp, scale=-0.5).then_inc(root_ready, 1)
                    roots += 1
                if what in ("norm1", "norm2"):
                    base, dst = (0, mh) if what == "norm1" else (KD, hh)
                    for k in range(KD):
                        if what == "norm1" and k in (0, 4):
                            split_hi(2 + k // 4, 2 + k // 4, 2)
                        act.wait_ge(h_ready, base + k + 1)
                        if what == "norm2" and k == 0:
                            act.wait_ge(w_used, EARLY_W)
                        if what == "norm2" and k in (0, 4):
                            n = EARLY_W + 2 + k // 4
                            split_hi(n, n, n // RAW + 1)
                        act.activation(dst[:, k, :], zc[:, k % 2, :], ACT.Copy).then_inc(h_hi, 1)
                if what == "early":
                    act.sem_inc(out_done, FREE_BANKS)
                    act.sem_inc(sc_ready, FREE_BANKS)
                    for j in range(2):
                        act.sem_inc(a_out[j], FREE_A)
                    for i in range(UP_EARLY):
                        if i % 2 == 0:
                            n = QUERY_W + i // 2
                            split_hi(n, n, n // RAW + 1)
                        act.wait_ge(early_scaled, i + 1)
                        act.wait_ge(a_out[i % 2], 16 * (i // 2) + FREE_A)
                        act.activation(act_a[:, i % 2, :], bank[S_BANK + i][:, :], ACT.Gelu).then_inc(early_done, 1)
                        act.wait_ge(early_done, i + 1)
                        act.dma_start(a_dram[i], act_a[:, i % 2, :]).then_inc(a_out[i % 2], 16)
                    act.dma_start(keys[:, :, :], keysT).then_inc(in_keys, 16)

            def next_hi(n, static, rounds):
                split_hi(n + 2, static + 2, rounds + ((static + 2) // RAW + 1))

            def gelu(n, static, slot):
                act.wait_ge(w_used, n + 1)
                act.activation(act_a[:, slot, :], bank[static % 2][:, :], ACT.Gelu).then_inc(out_done, 1)

            def up_stored(n, static, rounds, turn, j):
                act.wait_ge(a_out[j], turn * 16 + FREE_A)
                gelu(n, static, j)
                next_hi(n, static, rounds)
                act.wait_ge(out_done, n + (FREE_BANKS + 1 - QUERY_W))
                act.dma_start(a_dram[bass.ds(turn * 2 + j, 1)].rearrange("a p n -> p (a n)"), act_a[:, j, :])\
                   .then_inc(a_out[j], 16)

            with act.Fori(0, ROUNDS) as it:
                for k in range(ROUND_Q):
                    n = QUERY_W + 3 * k
                    rounds = it * (ROUND_W // RAW)
                    act.wait_ge(w_used, it * ROUND_W + (n + 1))
                    act.activation(qh[:, k % 2, :], bank[n % 2][:, :], ACT.Copy).then_inc(out_done, 1)
                    next_hi(it * ROUND_W + n, n, rounds)
                    turn = it * (ROUND_U // 2) + (UP_EARLY // 2 + k)
                    up_stored(it * ROUND_W + (n + 1), n + 1, rounds, turn, 0)
                    act.wait_ge(sc_prod, it * ROUND_Q + (k + 1))
                    act.wait_ge(sc_used, it * ROUND_Q + (k + 1))
                    act.activation(sc[:, k, :, :].rearrange("p b k -> p (b k)"), bank[S_BANK + k % 2][:, :], ACT.Copy)\
                       .then_inc(sc_ready, 1)
                    up_stored(it * ROUND_W + (n + 2), n + 2, rounds, turn, 1)

            def ups_stored(first, turns):
                with act.Fori(0, turns) as it:
                    for j in range(2):
                        up_stored(it * 2 + (first + j), first + j, it, it + (first - U_LAG) // 2, j)

            ups_stored(SOFT_W, SOFT_TURNS[0])
            act.wait_ge(gd_ready, 1)
            act.activation(ge[:, :, :, :], best[:, :, :, :], ACT.Exp).then_inc(ge_ready, 1)
            ups_stored(SOFT_W + 2 * SOFT_TURNS[0], SOFT_TURNS[1])
            for a in range(3):
                act.wait_ge(tr_ready, a + 1)
                act.activation(slotT[:, a, :], bank[PT_BANK + a % 2][:, :], ACT.Copy).then_inc(tr_saved, 1)
            ups_stored(SOFT_W + 2 * sum(SOFT_TURNS[:2]), SOFT_TURNS[2])

            act.sem_inc(gp_used, FREE_BANKS)
            for b in range(TB):
                if b >= 2:
                    act.wait_ge(gp_stored[b % 2], 16 * PIECES)
                with act.Fori(0, GATE_TURNS) as it:
                    for j in range(2):
                        for k in range(GROUPS):
                            group = GROUPS * j + k
                            act.wait_ge(oh_used, it * (2 * GROUPS) + (FREE_OH + P // GROUP * b + group + 1))
                            act.activation(gbuf[:, b % 2, :, bass.ds(it * (2 * GROUPS * GROUP) + GROUP * group, GROUP)],
                                           bank[GP + k % 2][:, :].rearrange("j (t i) -> j i t", t=GROUP), ACT.Copy)\
                               .then_inc(gp_used, 1)
                        n = GATE_W + 2 * GATE_TURNS * b + j
                        up_stored(it * 2 + n, n, it, it + (n - j - U_LAG) // 2, j)
            ups_stored(REST_W, UP_REST // 2)

            for j in range(2):
                act.wait_ge(a_out[j], FREE_A + 16 * (STORED // 2))

            def split_v(it, g, j):
                s = 2 * g + j
                act.wait_ge(vraw_in[j], it * 32 + 16 * (g + 1))
                act.wait_ge(y_ready, it * 16 + KD * (g + 1))
                act.activation(vh[:, s, :], vraw[:, j, :], ACT.Copy).then_inc(v_hi, 1)

            def body(it, last=False):
                split_v(it, 0, 0)
                split_v(it, 0, 1)
                for j in range(2):
                    act.wait_ge(w_ready, it * 4 + (j + 1))
                    gelu(it * 2 + (EXP_W + j), EXP_W + j, j)
                    if not last:
                        next_hi(it * 2 + (EXP_W + j), EXP_W + j, it)
                split_v(it, 1, 0)
                split_v(it, 1, 1)

            with act.Fori(0, BODIES - 1) as it:
                body(it)
            body(BODIES - 1, last=True)

        @block.tensor
        def _(pe):
            def three(dst, ah, al, bh, bl, start, stop):
                pe.matmul(dst, ah, bh, start=start, stop=False)
                pe.matmul(dst, ah, bl, start=False, stop=False)
                return pe.matmul(dst, al, bh, start=False, stop=stop)

            def project(dst, s, right_h, right_l, between=None, order=range(KD)):
                for k in order:
                    if between is not None:
                        between(k)
                    last = three(dst, wh[:, s, k * P:(k + 1) * P], wl[:, s, k * P:(k + 1) * P],
                                 right_h[:, k, :], right_l[:, k, :], k == order[0], k == order[-1])
                last.then_inc(w_used, 1)

            def sum_square(i, weights, start, stop):
                pe.wait_ge(sq_ready, i + 1)
                pe.matmul(bank[SS][:, :], weights, sq[:, i % 4, :], start=start, stop=stop).then_inc(sq_used, 1)

            pe.wait_ge(in_consts, 32)
            last_in_bank = {}

            def run(what, i, inner):
                if what == "norm1":
                    for k in range(KD):
                        sum_square(k, ones, k == 0, k == KD - 1)
                        if k == 3:
                            run("proj", VALUES[0], [])
                elif what == "columns":
                    pe.wait_ge(col_ready, 1)
                    for b in range(TB):
                        last = pe.transpose(bank[SS][:, b * P:(b + 1) * P], rinv[:, b * P:(b + 1) * P], ident)
                    last.then_inc(col_prod, 1)
                elif what == "proj":
                    n, kd = i, kind(i)
                    pe.wait_ge(w_lo, n + 1)
                    if kd == "v":
                        pair = VALUES.index(n)
                        pe.wait_ge(g_lo, 2 * pair + 2)
                        for b in range(TB):
                            for kk in range(2):
                                k = 2 * pair + kk
                                at, w = slice(b * P, (b + 1) * P), slice(kk * T, (kk + 1) * T)
                                last = three(bank[S_BANK + b][:, :], hh[:, k, at], hl[:, k, at],
                                             wh[:, n % SPLIT, w], wl[:, n % SPLIT, w], k == 0, k == KD - 1)
                        last.then_inc(w_used, 1)
                        return
                    if bank_of(n) in last_in_bank:
                        pe.wait_ge(*taken(last_in_bank[bank_of(n)]))
                    last_in_bank[bank_of(n)] = n

                    def between(k):
                        if n == F_W:
                            pe.wait_ge(h_lo, k + 1)
                        if n == OUT_W and k < 4:
                            pe.wait_ge(pool_lo, k + 1)
                        elif n == OUT_W:
                            pe.wait_ge(att_lo, 2 * (k - 4) + 2)
                        for at, w, j in inner:
                            if at == k:
                                run(w, j, [])

                    project(bank[bank_of(n)][:, :], n % SPLIT, *((hh, hl) if kd == "out" else (mh, ml)), between,
                            (4, 5, 6, 0, 1, 2, 3, 7) if n == OUT_W else range(KD))
                    if n > OUT_W:
                        sum_square(SQ_OUT + n - OUT_W - 1, ones, n == OUT_W + 1, False)
                elif what == "ss":
                    pe.wait_ge(var_ready, 1 + i)
                    pe.wait_ge(col_ready, 2)
                    sum_square(SQ_QK + i, block_ones, True, True)
                elif what == "poolmix":
                    pe.wait_ge(zc_used, 9 + i)
                    if i:
                        pe.wait_ge(pool_lo, i)
                    else:
                        pe.wait_ge(var_ready, 9)
                        pe.wait_ge(in_pool, 16)
                    pe.matmul(bank[SS][:, :], wp[:, i, :], pm[:, :], start=True, stop=True).then_inc(pool_prod, 1)
                elif what == "score":
                    h, b = i
                    c, m = h // 2, TB * h + b
                    rows = slice(DH * (h % 2), DH * (h % 2) + DH)
                    pe.wait_ge(zc_used, 2 * c + 2)
                    if m >= 2:
                        pe.wait_ge(s_masked, m - 1)
                    else:
                        pe.wait_ge(v_saved, TB)
                    pe.matmul(bank[S_BANK + m % 2][:, 0:(b + 1) * P], qn[rows, c, b * P:(b + 1) * P],
                              kn[rows, c, 0:(b + 1) * P], start=True, stop=True).then_inc(s_ready, 1)
                elif what == "transpose":
                    h, g = i
                    pieces = ([(0, b) for b in range(4)], [(1, b) for b in range(1, 4)], [(2, 2), (2, 3), (3, 3)])[g]
                    m = 3 * h + g
                    if m >= 2:
                        pe.wait_ge(pt_saved, m - 1)
                    for at, (key, b) in enumerate(pieces):
                        pe.wait_ge(p_scaled, TB * h + b + 1)
                        last = pe.transpose(bank[PT_BANK + m % 2][:, at * P:(at + 1) * P],
                                            pr[:, h % 2, b, key * P:(key + 1) * P], ident)
                    last.then_inc(pt_ready, 1)
                elif what == "pv":
                    h = i
                    pe.wait_ge(pt_saved, 3 * h + 3)
                    if h:
                        pe.wait_ge(att_lo, h)
                    for key in range(TB):
                        size = (TB - key) * P
                        last = pe.matmul(bank[PV][:, key * P:T], vs[:, key, (h // 2) * P:(h // 2 + 1) * P],
                                         pT[:, h % 2, KEY_AT[key]:KEY_AT[key] + size],
                                         start=(key == 0), stop=(key == TB - 1))
                    last.then_inc(pv_ready, 1)
                elif what == "norm2":
                    sum_square(SQ_OUT + KD - 1, ones, False, True)
                elif what == "early":
                    for j in range(UP_EARLY):
                        pe.wait_ge(w_lo, EARLY_W + j + 1)
                        project(bank[S_BANK + j][:, :], (EARLY_W + j) % SPLIT, mh, ml,
                                (lambda k: pe.wait_ge(g_lo, KD + k + 1)) if j == 0 else None)

            for stage in stages:
                if stage[:2] != ("proj", VALUES[0]):
                    run(*stage)

            pe.wait_ge(h_lo, 2 * KD)

            def turn(n, static, between=None):
                pe.wait_ge(w_lo, n + 1)
                pe.wait_ge(out_done, n + (1 - QUERY_W))
                project(bank[static % 2][:, :], static % SPLIT, hh, hl, between)

            def scores(it, k):
                pe.wait_ge(in_keys, 16)
                pe.wait_ge(early_done, UP_EARLY)
                pe.wait_ge(out_done, it * ROUND_W + (FREE_BANKS + 3 * k + 1))
                pe.wait_ge(sc_ready, it * ROUND_Q + (k + 1))
                for b in range(TB):
                    last = pe.matmul(bank[S_BANK + k % 2][:, b * P:(b + 1) * P], qh[:, k % 2, b * P:(b + 1) * P],
                                     keys[:, k % 2, :], start=True, stop=True)
                last.then_inc(sc_prod, 1)

            with pe.Fori(0, ROUNDS) as it:
                for k in range(ROUND_Q):
                    for j in range(3):
                        n = QUERY_W + 3 * k + j
                        turn(it * ROUND_W + n, n)
                        if j == 1:
                            scores(it, k)

            def turns(first, count):
                with pe.Fori(0, count) as it:
                    for j in range(2):
                        turn(it * 2 + (first + j), first + j)

            turns(SOFT_W, sum(SOFT_TURNS[:2]))
            pe.wait_ge(sel_ready, 1)
            for a in range(3):
                if a == 2:
                    pe.wait_ge(tr_saved, 1)
                for b in range(TB):
                    last = pe.transpose(bank[PT_BANK + a % 2][:, b * P:(b + 1) * P],
                                        sel[:, a, b, :, :].rearrange("p h k -> p (h k)"), ident)
                last.then_inc(tr_ready, 1)
            turns(SOFT_W + 2 * sum(SOFT_TURNS[:2]), SOFT_TURNS[2])

            pe.sem_inc(oh_used, FREE_OH)
            with pe.Fori(0, UP_GATE // 2) as it:
                for j in range(2):
                    def frames(k):
                        group = it * (2 * GROUPS) + (GROUPS * j + k)
                        pe.wait_ge(oh_ready, group + 1)
                        pe.wait_ge(gp_used, group + 1)
                        for t in range(GROUP):
                            last = pe.matmul(bank[GP + k % 2][:, t * P:(t + 1) * P], ohb[:, k % 2, t, :],
                                             oha[:, k % 2, t, :], start=True, stop=True)
                        last.then_inc(oh_used, 1)

                    turn(it * 2 + (GATE_W + j), GATE_W + j, frames)
            turns(REST_W, UP_REST // 2)

            pe.sem_inc(y_ready, FREE_Y)

            def down(it, g):
                pe.wait_ge(w_ready, it * 4 + (FREE_W + 2 * g + 2))
                pe.wait_ge(v_lo, it * 4 + (FREE_V + 2 * g + 2))
                for m in range(KD):
                    pe.wait_ge(y_added, it * 16 + (KD * g + m - 3 + FREE_SUM))
                    for j in range(2):
                        s, at_ = 2 * g + j, slice(m * P, (m + 1) * P)
                        last = three(bank[4 + m % 4][:, :], vh[:, s, at_], vl[:, s, at_], Wh[:, s, :], Wl[:, s, :],
                                     j == 0, j == 1)
                    last.then_inc(y_ready, 1)

            with pe.Fori(0, BODIES) as it:
                for j in range(2):
                    turn(it * 2 + (EXP_W + j), EXP_W + j)
                down(it, 0)
                down(it, 1)

        @block.vector
        def _(dve):
            base, count = 0, 0

            def lo_part(i, k, hi_done, lo_done, high, low):
                dve.wait_ge(hi_done, i + 1)
                dve.tensor_tensor(low[:, k, :], zc[:, k % 2, :], high[:, k, :].bitcast(F32), ALU.subtract)\
                   .then_inc(lo_done, 1)

            def step(instruction):
                nonlocal count
                count += 1
                instruction.then_inc(dve_done, 1)

            def fence():
                dve.wait_ge(dve_done, base + count)

            def fence_apart():
                dve.drain()

            for i in range(3):
                step(dve.memset(pad[:, i, 0:PAD], 0.0))
            dve.wait_ge(in_consts, 32)
            roots = 0

            def times_gain(i, g, high, low):
                k = i % KD
                if i % KD >= 2:
                    dve.wait_ge(g_lo, i - 1)
                dve.tensor_scalar(zc[:, k % 2, :], x[:, k, :], vec[:, g + k:g + k + 1], None, ALU.mult)\
                   .then_inc(g_ready, 1)
                lo_part(i, k, g_hi, g_lo, high, low)

            for what, i in in_turn:
                if what == "norm1":
                    for k in range(KD):
                        dve.wait_ge(in_x[k // 2], 16)
                        times_gain(k, G1, hh, hl)
                if what in ("norm1", "ss", "norm2"):
                    scale, eps = {"norm1": (1.0 / D, EPS), "norm2": (1.0 / D, EPS),
                                  "ss": (1.0, DH * EPS) if i % 2 == 0 else (1.0 / DH, EPS)}[what]
                    dve.wait_ge(sq_used, {"norm1": KD, "ss": SQ_QK + i + 1, "norm2": 3 * KD}[what])
                    fence()
                    dve.tensor_scalar(var[:, :], bank[SS][:, :], scale, eps, ALU.mult, ALU.add).then_inc(var_ready, 1)
                if what in ("norm1", "norm", "norm2"):
                    dve.wait_ge(root_ready, roots + 1)
                    roots += 1
                    step(dve.scalar_tensor_tensor(newt[:, :], root[:, :], -0.5, root[:, :], ALU.mult, ALU.mult))
                    fence()
                    step(dve.tensor_tensor(newt[:, :], newt[:, :], var[:, :], ALU.mult))
                    fence()
                    step(dve.scalar_tensor_tensor(rinv[:, :], newt[:, :], 1.5, root[:, :], ALU.add, ALU.mult))
                    fence()
                if what == "norm1":
                    dve.sem_inc(col_ready, 1)
                if what == "norm":
                    n, c = i, i // 2
                    dst, g = (qn, QG) if i % 2 == 0 else (kn, KG)
                    dve.scalar_tensor_tensor(dst[:, c, :], zc[:, n % 2, :], vec[:, g + c:g + c + 1], rinv[:, :],
                                             ALU.mult, ALU.mult).then_inc(zc_used, 1)
                    dve.wait_ge(zc_used, i + 1)
                elif what in ("norm1", "norm2"):
                    first, g, high, low = (0, G1, mh, ml) if what == "norm1" else (KD, G2, hh, hl)
                    for k in range(KD):
                        if k >= 2:
                            dve.wait_ge(h_lo, first + k - 1)
                        else:
                            dve.wait_ge(g_lo, first + KD)
                        dve.scalar_tensor_tensor(zc[:, k % 2, :], x[:, k, :], vec[:, g + k:g + k + 1], rinv[:, :],
                                                 ALU.mult, ALU.mult).then_inc(h_ready, 1)
                        if k:
                            lo_part(first + k - 1, k - 1, h_hi, h_lo, high, low)
                    lo_part(first + KD - 1, KD - 1, h_hi, h_lo, high, low)
                elif what == "early":
                    for i in range(UP_EARLY):
                        dve.wait_ge(w_used, EARLY_W + i + 1)
                        dve.tensor_tensor(bank[S_BANK + i][:, :], bank[S_BANK + i][:, :], rinv[:, :], ALU.mult)\
                           .then_inc(early_scaled, 1)
                elif what == "proj":
                    n, kd = i, kind(i)
                    if kd == "f":
                        dve.wait_ge(w_used, F_W + 1)
                        dve.tensor_scalar(fg[:, 0, :], bank[bank_of(n)][0:HEADS, :], vec[0:HEADS, BF:BF + 1], None,
                                          ALU.add).then_inc(f_taken, 1)
                        dve.wait_ge(f_taken, 1)
                        dve.scalar_tensor_tensor(fg[:, 1, :], fg[:, 0, :], -1.0, fg[:, 0, :], ALU.mult, ALU.min)\
                           .then_inc(f_abs, 1)
                        dve.wait_ge(f_ln, 2)
                        step(dve.scalar_tensor_tensor(fg[:, 0, :], fg[:, 0, :], 0.0, fg[:, 1, :],
                                                      ALU.min, ALU.subtract))
                        fence()
                        step(dve.tensor_scalar(fg[:, 0, :], fg[:, 0, :], -1.0, None, ALU.mult))
                        fence()
                        dve.tensor_tensor_scan(fg[:, 2, :], fg[:, 0, :], fg[:, 1, :], 0.0, ALU.add, ALU.bypass)\
                           .then_inc(f_done, 1)
                    elif kd == "out":
                        m = n - OUT_W
                        dve.wait_ge(w_used, n + 1)
                        dve.tensor_tensor(x[:, m, :], x[:, m, :], bank[bank_of(n)][:, :], ALU.add)\
                           .then_inc(x1_ready, 1)
                        if m == 0:
                            dve.wait_ge(zc_used, 12)
                        dve.wait_ge(x1_ready, m + 1)
                        times_gain(KD + m, G2, mh, ml)
                elif what == "columns":
                    dve.wait_ge(col_prod, 1)
                    dve.tensor_copy(rcol[:, :], bank[SS][:, :].rearrange("p (b t) -> p b t", b=TB)[:, :, 0])\
                       .then_inc(col_ready, 1)
                    dve.wait_ge(col_ready, 2)
                    for b in range(TB):
                        dve.tensor_scalar(vs[:, b, :], bank[S_BANK + b][:, :], rcol[:, b:b + 1], None, ALU.mult)\
                           .then_inc(v_saved, 1)
                elif what == "mean":
                    g, z = i, len(QK_W) + i
                    w = WINDOWS[g]
                    dve.wait_ge(zc_ready, z + 1)
                    fence()
                    step(dve.tensor_copy(pad[:, 0, PAD:], zc[:, z % 2, :]))
                    src, s = 0, 1
                    while s < w:
                        fence()
                        dst = 2 if src == 1 else 1
                        step(dve.tensor_tensor(pad[:, dst, PAD:], pad[:, src, PAD:],
                                               pad[:, src, PAD - s:PAD + T - s], ALU.add))
                        src, s = dst, 2 * s
                    fence()
                    if g:
                        dve.wait_ge(pool_prod, g)
                    step(dve.scalar_tensor_tensor(pm[:, :], pad[:, src, PAD:], 1.0 / w, zc[:, z % 2, :],
                                                  ALU.mult, ALU.subtract))
                    fence()
                    step(dve.tensor_tensor(pm[:, 0:PAD], pad[:, src, PAD:2 * PAD],
                                           cst[:, C_CNT + PAD * g:C_CNT + PAD * (g + 1)], ALU.mult))
                    fence()
                    dve.tensor_tensor(pm[:, 0:PAD], pm[:, 0:PAD], zc[:, z % 2, 0:PAD], ALU.subtract)\
                       .then_inc(zc_used, 1)
                elif what == "poolmix":
                    dve.wait_ge(pool_hi, i + 1)
                    dve.scalar_tensor_tensor(hl[:, i, :], bank[SS][:, :], vec[:, PS + i:PS + i + 1],
                                             hh[:, i, :].bitcast(F32), ALU.mult, ALU.subtract).then_inc(pool_lo, 1)
                elif what == "score":
                    h, b = i
                    s = bank[S_BANK + (TB * h + b) % 2]
                    size = (b + 1) * P
                    if b == 0:
                        dve.wait_ge(nf_in[h % 2], 16 * (h // 2 + 1))
                        if h >= 2:
                            dve.wait_ge(pt_ready, 3 * (h - 1))
                    dve.wait_ge(s_ready, TB * h + b + 1)
                    step(dve.tensor_tensor(s[:, b * P:size], s[:, b * P:size], mask, ALU.add))
                    fence()
                    step(dve.tensor_tensor_reduce(pr[:, h % 2, b, 0:size], s[:, 0:size], nf[:, h % 2, 0:size],
                                                  1.0, LOWEST, ALU.add, ALU.max, rmax[:, h % 2, b:b + 1]))
                    fence()
                    dve.tensor_scalar(nmax[:, h % 2, b:b + 1], rmax[:, h % 2, b:b + 1], -1.0, None, ALU.mult)\
                       .then_inc(s_masked, 1)
                elif what == "scale":
                    h, b = i
                    size = (b + 1) * P
                    dve.wait_ge(e_ready, TB * h + b + 1)
                    step(dve.reciprocal(rrec[:, h % 2, b:b + 1], rsum[:, h % 2, b:b + 1]))
                    fence()
                    dve.tensor_scalar(pr[:, h % 2, b, 0:size], pr[:, h % 2, b, 0:size], rrec[:, h % 2, b:b + 1],
                                      None, ALU.mult).then_inc(p_scaled, 1)
                elif what == "pv":
                    rows = slice(DH * (i % 2), DH * (i % 2) + DH)
                    dve.wait_ge(att_hi, i + 1)
                    dve.tensor_tensor(hl[rows, 4 + i // 2, :], bank[PV][rows, :],
                                      hh[rows, 4 + i // 2, :].bitcast(F32), ALU.subtract).then_inc(att_lo, 1)

            dve.sem_inc(sc_used, FREE_SC)
            fence()
            before = count
            with dve.Fori(0, ROUNDS) as it:
                base, count = it * RETRIEVE_STEPS + before, 0
                for k in range(4):
                    half = k % 2
                    kt, ku_ = kv[:, half], ku[:, half]
                    s = sc[:, k]
                    dve.wait_ge(sc_ready, it * ROUND_Q + (FREE_BANKS + k + 1))
                    dve.memset(tick[:, :], 0.0)
                    fence_apart()
                    for b in range(TB):
                        step(dve.max(kt[:, b, 0:8], s[:, b, :]))
                    fence_apart()
                    for b in range(TB):
                        step(dve.max_index(ku_[:, b, 0:8], kt[:, b, 0:8], s[:, b, :]))
                        step(dve.match_replace(sc2[:, b, :], kt[:, b, 0:8], s[:, b, :], LOWEST))
                    fence_apart()
                    for b in range(TB):
                        ins = dve.max(kt[:, b, 8:16], sc2[:, b, :])
                        step(ins)
                    fence_apart()
                    for b in range(TB):
                        ins = dve.max_index(ku_[:, b, 8:16], kt[:, b, 8:16], sc2[:, b, :])
                        if b < TB - 1:
                            step(ins)
                        else:
                            ins.then_inc(sc_used, 1)
                    if half == 0:
                        continue
                    h = it * 2 + k // 2
                    dve.wait_ge(sc_used, it * 4 + (FREE_SC + k + 1))
                    wide = [P, TB, TOPK, TOPK]
                    step(dve.tensor_tensor(cand[:, :, :, :], kv[:, 0].unsqueeze(3).broadcast_to(wide),
                                           kv[:, 1].unsqueeze(2).broadcast_to(wide), ALU.add))
                    step(dve.tensor_copy(kf[:, :, :, :], ku[:, :, :, :]))
                    fence_apart()
                    flat = cand[:, :, :, :].rearrange("p b i j -> p b (i j)")
                    for b in range(TB):
                        step(dve.max(tv[:, b, 0:8], flat[:, b, :]))
                    fence_apart()
                    for b in range(TB):
                        step(dve.max_index(pos[:, b, 0:8], tv[:, b, 0:8], flat[:, b, :]))
                        step(dve.match_replace(cand2[:, b, :], tv[:, b, 0:8], flat[:, b, :], LOWEST))
                    fence_apart()
                    for b in range(TB):
                        step(dve.max(tv[:, b, 8:16], cand2[:, b, :]))
                    fence_apart()
                    for b in range(TB):
                        step(dve.max_index(pos[:, b, 8:16], tv[:, b, 8:16], cand2[:, b, :]))
                    fence()
                    step(dve.tensor_copy(best[:, :, bass.ds(h, 1), :].rearrange("p b a k -> p b (a k)"), tv[:, :, :]))
                    step(dve.tensor_scalar(ab[:, 0], pos[:, :, :], 4, None, ALU.logical_shift_right))
                    step(dve.tensor_scalar(ab[:, 1], pos[:, :, :], 15, None, ALU.bitwise_and))
                    fence()
                    step(dve.tensor_copy(abf[:, :, :, :], ab[:, :, :, :]))
                    fence()
                    for a in range(2):
                        step(dve.tensor_tensor(hit[:, a], abf[:, a].unsqueeze(3).broadcast_to(wide),
                                               iota[:, 0:TOPK].unsqueeze(1).unsqueeze(1).broadcast_to(wide),
                                               ALU.is_equal))
                    fence()
                    for a in range(2):
                        step(dve.tensor_tensor(hit2[:, a], hit[:, a], kf[:, a].unsqueeze(2).broadcast_to(wide),
                                               ALU.mult))
                    fence()
                    for a in range(2):
                        step(dve.tensor_reduce(sel[:, a, :, bass.ds(h, 1), :].rearrange("p b a k -> p b (a k)"),
                                               hit2[:, a], AX.X, ALU.add))
                assert count == RETRIEVE_STEPS, count
            base, count = 0, before + RETRIEVE_STEPS * ROUNDS
            fence()
            narrow = [P, TB * PH, TOPK]
            flat_best, flat_e = (a[:, :, :, :].rearrange("p b h k -> p (b h) k") for a in (best, ge))
            flat_s, flat_r = (a[:, :, :].rearrange("p b h -> p (b h)") for a in (gs, gr))
            step(dve.tensor_copy(flat_s, flat_best[:, :, 0:1].rearrange("p n a -> p (n a)")))
            fence()
            dve.tensor_tensor(flat_best, flat_best, flat_s.unsqueeze(2).broadcast_to(narrow), ALU.subtract)\
               .then_inc(gd_ready, 1)
            dve.wait_ge(ge_ready, 1)
            step(dve.tensor_reduce(flat_s, flat_e, AX.X, ALU.add))
            fence()
            step(dve.reciprocal(flat_r, flat_s))
            fence()
            dve.tensor_tensor(sel[:, 2, :, :, :].rearrange("p b h k -> p (b h) k"), flat_e,
                              flat_r.unsqueeze(2).broadcast_to(narrow), ALU.mult).then_inc(sel_ready, 1)

            dve.wait_ge(tr_saved, 3)
            with dve.Fori(0, T // 8) as it:
                for k in range(2):
                    dve.wait_ge(oh_used, it * 2 + (k + 1))
                    at = bass.ds(it * 8 + 4 * k, 4)
                    dve.tensor_tensor(ohb[:, k], iota.unsqueeze(1).broadcast_to([P, 4, P]),
                                      slotT[:, 1, at].unsqueeze(2).broadcast_to([P, 4, P]), ALU.is_equal)
                    for t in range(4):
                        one = bass.ds(it * 8 + (4 * k + t), 1)
                        last = dve.tensor_scalar(oha[:, k, t, :], iota, slotT[:, 0, one], slotT[:, 2, one],
                                                 ALU.is_equal, ALU.mult)
                    last.then_inc(oh_ready, 1)

            dve.sem_inc(y_added, FREE_SUM)
            dve.sem_inc(w_ready, FREE_W)
            before = count

            def weigh(it, g, j):
                s = 2 * g + j
                if g == 0:
                    dve.wait_ge(at_in[j], it * 16 + 16)
                    a = old_a[:, j, :]
                else:
                    dve.wait_ge(out_done, it * 2 + (FREE_BANKS + EXP_W - QUERY_W + j + 1))
                    a = act_a[:, j, :]
                dve.wait_ge(gt_in[j], it * 32 + 16 * (g + 1))
                dve.wait_ge(w_ready, it * 4 + (s + 1))
                dve.tensor_tensor(wf[:, j, :], gt[:, j, :], a, ALU.mult).then_inc(dve_done, 1)
                dve.wait_ge(y_ready, it * 16 + KD * (g + 1))
                dve.wait_ge(dve_done, it * 8 + (before + 2 * s + 1))
                dve.tensor_copy(Wh[:, s, :], wf[:, j, :]).then_inc(dve_done, 1)
                dve.wait_ge(dve_done, it * 8 + (before + 2 * s + 2))
                dve.tensor_tensor(Wl[:, s, :], wf[:, j, :], Wh[:, s, :].bitcast(F32), ALU.subtract)\
                   .then_inc(w_ready, 1)

            def add_up(it, g):
                for m in range(KD):
                    dve.wait_ge(y_ready, it * 16 + (FREE_Y + KD * g + m + 1))
                    dve.wait_ge(y_added, it * 16 + (KD * g + m + 1))
                    dve.tensor_tensor(x[:, m, :], x[:, m, :], bank[4 + m % 4][:, :], ALU.add).then_inc(y_added, 1)

            with dve.Fori(0, BODIES) as it:
                for g in range(2):
                    weigh(it, g, 0)
                    weigh(it, g, 1)
                add_up(it, 0)
                add_up(it, 1)


RETRIEVE_STEPS = 2 * (2 * (4 + 8 + 4 + 3) + 2 + 4 + 8 + 4 + 4 + 3 + 1 + 2 + 2 + 2)

_OUT = "out_dram"


def _constants(np):
    c = np.zeros((P, N_CONST), np.float32)
    p = np.arange(P)
    c[:, C_ID:C_ID + P] = np.eye(P)
    c[:, C_MASK:C_MASK + P] = np.where(p[None, :] <= p[:, None], 0.0, -1.0e30)
    c[:, C_IOTA:C_IOTA + P] = p[None, :]
    c[:, C_BLOCK:C_BLOCK + P] = p[:, None] // DH == p[None, :] // DH
    c[:, C_ONES:C_ONES + P] = 1.0
    for g, w in enumerate(WINDOWS):
        c[:, C_CNT + PAD * g:C_CNT + PAD * (g + 1)] = 1.0 / np.minimum(np.arange(PAD) + 1, w)
    c[:, C_EPS] = 1.0
    return c


def kernel(x, norm1_g, w_in, b_forget, q_norm_g, k_norm_g, w_pool, pool_scale, w_out,
           norm2_g, w_query, peer_sub_keys, expert_u, expert_v):
    import numpy as np
    import concourse.bacc as bacc
    from concourse.bass_utils import run_bass_kernel_spmd

    a = {n: np.asarray(v) for n, v in dict(x=x, n1=norm1_g, wi=w_in, bf=b_forget, qg=q_norm_g, kg=k_norm_g,
                                           wp=w_pool, ps=pool_scale, wo=w_out, n2=norm2_g, wq=w_query,
                                           sk=peer_sub_keys, u=expert_u, v=expert_v).items()}

    def column_chunks(w):
        n = w.shape[1] // P
        return w.reshape(KD, P, n, P).transpose(2, 1, 0, 3).reshape(n, P, KD * P)

    wi = a["wi"][0]
    forget = np.concatenate([wi[:, 4 * T:], np.zeros((D, P - HEADS), wi.dtype)], axis=1)
    cols = column_chunks(wi[:, :4 * T])
    values = wi[:, 3 * T:4 * T].reshape(4, 2, P, T).transpose(0, 2, 1, 3).reshape(4, P, 2 * T)
    qk = [cols[o + c] for c in range(4) for o in (4, 8)]
    wst = np.concatenate([values, column_chunks(forget), qk, cols[0:4], column_chunks(a["wo"][0]),
                          column_chunks(a["wq"][0])])
    per_channel = [a["n1"][0].reshape(8, P).T, a["n2"][0].reshape(8, P).T, a["qg"][0].reshape(4, P).T,
                   a["kg"][0].reshape(4, P).T, a["ps"][0].reshape(4, P).T,
                   np.pad(a["bf"][0], (0, P - HEADS))[:, None]]
    ins = {
        "xT": a["x"][0].T.reshape(KD, P, T).transpose(1, 0, 2),
        "wst": wst,
        "vecs": np.concatenate(per_channel, axis=1),
        "consts": _constants(np),
        "w_pool": a["wp"][0].transpose(1, 0, 2),
        "keysT": a["sk"][0].transpose(2, 0, 1),
        "uT": a["u"][0].reshape(NCH, P, KD, P).transpose(0, 3, 2, 1).reshape(NCH, P, D),
        "v": a["v"][0].reshape(NCH, P, D),
    }
    ins = {n + "_dram": np.ascontiguousarray(v) for n, v in ins.items()}
    nc = bacc.Bacc("TRN2", target_bir_lowering=False, num_devices=1,
                   dynamic_dma_scratch_size=1024)
    aps = [nc.dram_tensor(n, v.shape, mybir.dt.from_np(v.dtype), kind="ExternalInput").ap() for n, v in ins.items()]
    aps.append(nc.dram_tensor(_OUT, (P, KD, T), F32, kind="ExternalOutput").ap())
    program(nc, *aps)
    got = run_bass_kernel_spmd(nc, [ins], core_ids=[0]).results[0][_OUT]
    return got.transpose(1, 0, 2).reshape(D, T).T.reshape(1, T, D)
```
